# Optimizing a Trainium2 kernel written in Bass

```python
import jax, jax.numpy as jnp
from jax import lax
import numpy as np

D_MODEL = 2048
BATCH = 1
SEQ = 256
DEPTH = 2

CHUNK = 64
HEAD_DIM = 64
MIX_WIDTH = D_MODEL
N_GROUPS = 4
GROUP_WIDTH = MIX_WIDTH // N_GROUPS
N_SB_HEADS = 4
SB_HEAD_DIM = GROUP_WIDTH // N_SB_HEADS
SB_QBLOCK = 128
N_SWA_HEADS = GROUP_WIDTH // HEAD_DIM
N_SWA_KV_HEADS = 2
SWA_KV_WIDTH = N_SWA_KV_HEADS * HEAD_DIM
SWA_WINDOW = 128
SWA_PREV_CHUNKS = SWA_WINDOW // CHUNK - 1
N_CA_HEADS = GROUP_WIDTH // HEAD_DIM
CA_PREV_CHUNKS = 8
MAX_REL_DIST = 128
N_REL = 2 * MAX_REL_DIST + 1
CONV_CHANNELS = GROUP_WIDTH
CONV_WIDTH = 31
N_MEM = 256
N_XATTN_HEADS = 4
XATTN_HEAD_DIM = 128
XATTN_WIDTH = N_XATTN_HEADS * XATTN_HEAD_DIM
D_FF = -(-8 * D_MODEL // (3 * 256)) * 256
ROPE_THETA = 10000.0
EPS = 1e-6
NEG_INF = -1e30
IN_SPLITS = (GROUP_WIDTH, GROUP_WIDTH, GROUP_WIDTH,
             GROUP_WIDTH, SWA_KV_WIDTH, SWA_KV_WIDTH,
             GROUP_WIDTH, GROUP_WIDTH, GROUP_WIDTH,
             2 * CONV_CHANNELS)
D_IN = sum(IN_SPLITS)

kernel_name = "hybrid_chunk_causal_parallel_groups"

def rmsnorm(x, g):
    xf = x.astype(jnp.float32)
    y = xf * lax.rsqrt(jnp.mean(xf * xf, axis=-1, keepdims=True) + EPS)
    return (y * g.astype(jnp.float32)).astype(x.dtype)

def rope(x, positions):
    d = x.shape[-1]
    half = d // 2
    inv = ROPE_THETA ** (-jnp.arange(half, dtype=jnp.float32) / half)
    ang = positions.astype(jnp.float32)[..., None] * inv
    cos = jnp.cos(ang)[:, :, None, :]
    sin = jnp.sin(ang)[:, :, None, :]
    xf = x.astype(jnp.float32)
    x1, x2 = xf[..., :half], xf[..., half:]
    return jnp.concatenate([x1 * cos - x2 * sin, x2 * cos + x1 * sin], axis=-1).astype(x.dtype)

def stick_breaking_attention(q, k, v):
    B, S, H, d = q.shape
    Q = SB_QBLOCK
    nb = S // Q
    scale = d ** -0.5
    qh = q.transpose(0, 2, 1, 3)
    kh = k.transpose(0, 2, 1, 3)
    vh = v.transpose(0, 2, 1, 3)
    tri_in = (jnp.arange(Q)[:, None] > jnp.arange(Q)[None, :]).astype(jnp.float32)
    outs = []
    for i in range(nb):
        nk = i + 1
        L = nk * Q
        qi = qh[:, :, i * Q:(i + 1) * Q]
        ki = kh[:, :, :L]
        vi = vh[:, :, :L]
        z = jnp.einsum('bhqd,bhsd->bhqs', qi, ki).astype(jnp.float32) * scale
        causal = jnp.arange(L)[None, :] < (i * Q + jnp.arange(Q))[:, None]
        ls = jax.nn.log_sigmoid(z)
        l1m = jnp.where(causal, ls - z, 0.0).reshape(B, H, Q, nk, Q)
        within = jnp.einsum('bhqnj,js->bhqns', l1m, tri_in)
        tot = jnp.sum(l1m, axis=-1)
        tri_blk = (jnp.arange(nk)[:, None] > jnp.arange(nk)[None, :]).astype(jnp.float32)
        later = jnp.einsum('bhqn,nm->bhqm', tot, tri_blk)
        logw = (ls.reshape(B, H, Q, nk, Q) + within + later[..., None]).reshape(B, H, Q, L)
        w = jnp.where(causal, jnp.exp(logw), 0.0)
        outs.append(jnp.einsum('bhqs,bhsd->bhqd', w.astype(vi.dtype), vi))
    out = jnp.concatenate(outs, axis=2)
    return out.transpose(0, 2, 1, 3).reshape(B, S, H * d)

def chunk_band_attention(q, k, v, n_prev, rel_bias=None, sinks=None):
    B, S, H, d = q.shape
    KVH = k.shape[2]
    G = H // KVH
    NC = S // CHUNK
    pad = n_prev * CHUNK
    band = pad + CHUNK
    scale = d ** -0.5
    kp = jnp.pad(k, ((0, 0), (pad, 0), (0, 0), (0, 0)))
    vp = jnp.pad(v, ((0, 0), (pad, 0), (0, 0), (0, 0)))
    qc = q.reshape(B, NC, CHUNK, KVH, G, d).transpose(1, 0, 3, 4, 2, 5)
    if rel_bias is not None:
        rel = (jnp.arange(CHUNK)[:, None] + pad) - jnp.arange(band)[None, :]
        rel_idx = jnp.clip(rel, -MAX_REL_DIST, MAX_REL_DIST) + MAX_REL_DIST
        bias = rel_bias[:, rel_idx].astype(jnp.float32).reshape(KVH, G, CHUNK, band)
    if sinks is not None:
        sink = sinks.astype(jnp.float32).reshape(KVH, G)[None, :, :, None, None]

    def one_chunk(args):
        qi, c = args
        start = c * CHUNK
        kb = lax.dynamic_slice_in_dim(kp, start, band, axis=1)
        vb = lax.dynamic_slice_in_dim(vp, start, band, axis=1)
        s = jnp.einsum('bkgqd,bskd->bkgqs', qi, kb).astype(jnp.float32) * scale
        if rel_bias is not None:
            s = s + bias[None]
        valid = (start - pad + jnp.arange(band)) >= 0
        s = jnp.where(valid, s, NEG_INF)
        if sinks is not None:
            m = jnp.maximum(jnp.max(s, axis=-1, keepdims=True), sink)
            p = jnp.exp(s - m)
            p = p / (jnp.sum(p, axis=-1, keepdims=True) + jnp.exp(sink - m))
        else:
            p = jax.nn.softmax(s, axis=-1)
        return jnp.einsum('bkgqs,bskd->bkgqd', p.astype(vb.dtype), vb)

    out = lax.map(one_chunk, (qc, jnp.arange(NC)))
    return out.transpose(1, 0, 4, 2, 3, 5).reshape(B, S, H * d)

def conformer_conv(u, dw_w, dw_b, ln_g, ln_b, pw_w, pw_b):
    a, gate = jnp.split(u, 2, axis=-1)
    h = a * jax.nn.sigmoid(gate)
    h = lax.conv_general_dilated(h, dw_w[:, None, :], window_strides=(1,),
                                 padding=[(CONV_WIDTH - 1, 0)],
                                 dimension_numbers=('NWC', 'WIO', 'NWC'),
                                 feature_group_count=CONV_CHANNELS) + dw_b
    hf = h.astype(jnp.float32)
    mu = jnp.mean(hf, axis=-1, keepdims=True)
    var = jnp.mean(jnp.square(hf - mu), axis=-1, keepdims=True)
    hf = (hf - mu) * lax.rsqrt(var + EPS) * ln_g.astype(jnp.float32) + ln_b.astype(jnp.float32)
    h = jax.nn.silu(hf).astype(u.dtype)
    return h @ pw_w + pw_b

def cross_attention(h, mem_n, w_xq, w_xkv, w_xo):
    B, S, _ = h.shape
    q = (h @ w_xq).reshape(B, S, N_XATTN_HEADS, XATTN_HEAD_DIM)
    kv = (mem_n @ w_xkv).reshape(B, N_MEM, 2, N_XATTN_HEADS, XATTN_HEAD_DIM)
    k, v = kv[:, :, 0], kv[:, :, 1]
    s = jnp.einsum('bqhd,bmhd->bhqm', q, k).astype(jnp.float32) * XATTN_HEAD_DIM ** -0.5
    p = jax.nn.softmax(s, axis=-1).astype(v.dtype)
    o = jnp.einsum('bhqm,bmhd->bqhd', p, v).reshape(B, S, XATTN_WIDTH)
    return o @ w_xo

def setup_inputs(seed: int = 0) -> dict:
    key = jax.random.key(seed)
    ks = jax.random.split(key, 24)

    def nrm(k, shape, scale):
        return jax.random.normal(k, shape, jnp.float32) * scale

    L = DEPTH
    offsets = jax.random.randint(ks[2], (BATCH, 1), 0, 4096, dtype=jnp.int32)
    positions = offsets + jnp.arange(SEQ, dtype=jnp.int32)[None, :]
    return {
        "x": nrm(ks[0], (BATCH, SEQ, D_MODEL), 1.0),
        "mem": nrm(ks[1], (BATCH, N_MEM, D_MODEL), 1.0),
        "positions": positions,
        "norm_mix_g": 1.0 + nrm(ks[3], (L, D_MODEL), 0.02),
        "w_in": nrm(ks[4], (L, D_MODEL, D_IN), D_MODEL ** -0.5),
        "swa_sinks": nrm(ks[5], (L, N_SWA_HEADS), 0.5),
        "ca_rel_bias": nrm(ks[6], (L, N_CA_HEADS, N_REL), 0.5),
        "conv_dw_w": nrm(ks[7], (L, CONV_WIDTH, CONV_CHANNELS), CONV_WIDTH ** -0.5),
        "conv_dw_b": nrm(ks[8], (L, CONV_CHANNELS), 0.02),
        "conv_ln_g": 1.0 + nrm(ks[9], (L, CONV_CHANNELS), 0.02),
        "conv_ln_b": nrm(ks[10], (L, CONV_CHANNELS), 0.02),
        "conv_pw_w": nrm(ks[11], (L, CONV_CHANNELS, CONV_CHANNELS), CONV_CHANNELS ** -0.5),
        "conv_pw_b": nrm(ks[12], (L, CONV_CHANNELS), 0.02),
        "group_norm_g": 1.0 + nrm(ks[13], (L, MIX_WIDTH), 0.02),
        "w_out": nrm(ks[14], (L, MIX_WIDTH, D_MODEL), MIX_WIDTH ** -0.5),
        "norm_xattn_g": 1.0 + nrm(ks[15], (L, D_MODEL), 0.02),
        "norm_mem_g": 1.0 + nrm(ks[16], (L, D_MODEL), 0.02),
        "w_xq": nrm(ks[17], (L, D_MODEL, XATTN_WIDTH), D_MODEL ** -0.5),
        "w_xkv": nrm(ks[18], (L, D_MODEL, 2 * XATTN_WIDTH), D_MODEL ** -0.5),
        "w_xo": nrm(ks[19], (L, XATTN_WIDTH, D_MODEL), XATTN_WIDTH ** -0.5),
        "norm_ffn_g": 1.0 + nrm(ks[20], (L, D_MODEL), 0.02),
        "w_gate_up": nrm(ks[21], (L, D_MODEL, 2 * D_FF), D_MODEL ** -0.5),
        "w_down": nrm(ks[22], (L, D_FF, D_MODEL), D_FF ** -0.5),
        "final_norm_g": 1.0 + nrm(ks[23], (D_MODEL,), 0.02),
    }

def reference(x, mem, positions, norm_mix_g, w_in, swa_sinks, ca_rel_bias, conv_dw_w, conv_dw_b,
              conv_ln_g, conv_ln_b, conv_pw_w, conv_pw_b, group_norm_g, w_out, norm_xattn_g,
              norm_mem_g, w_xq, w_xkv, w_xo, norm_ffn_g, w_gate_up, w_down, final_norm_g):
    B, S, _ = x.shape
    split_at = np.cumsum(IN_SPLITS)[:-1].tolist()
    for l in range(DEPTH):
        h = rmsnorm(x, norm_mix_g[l])
        u = h @ w_in[l]
        (qa, ka, va, qb, kb, vb, qc, kc, vc, ud) = jnp.split(u, split_at, axis=-1)
        heads = lambda t, n, hd: t.reshape(B, S, n, hd)
        ya = stick_breaking_attention(heads(qa, N_SB_HEADS, SB_HEAD_DIM),
                                      heads(ka, N_SB_HEADS, SB_HEAD_DIM),
                                      heads(va, N_SB_HEADS, SB_HEAD_DIM))
        yb = chunk_band_attention(rope(heads(qb, N_SWA_HEADS, HEAD_DIM), positions),
                                  rope(heads(kb, N_SWA_KV_HEADS, HEAD_DIM), positions),
                                  heads(vb, N_SWA_KV_HEADS, HEAD_DIM),
                                  SWA_PREV_CHUNKS, sinks=swa_sinks[l])
        yc = chunk_band_attention(heads(qc, N_CA_HEADS, HEAD_DIM), heads(kc, N_CA_HEADS, HEAD_DIM),
                                  heads(vc, N_CA_HEADS, HEAD_DIM),
                                  CA_PREV_CHUNKS, rel_bias=ca_rel_bias[l])
        yd = conformer_conv(ud, conv_dw_w[l], conv_dw_b[l], conv_ln_g[l], conv_ln_b[l],
                            conv_pw_w[l], conv_pw_b[l])
        y = jnp.stack([ya, yb, yc, yd], axis=2)
        y = rmsnorm(y, group_norm_g[l].reshape(N_GROUPS, GROUP_WIDTH)).reshape(B, S, MIX_WIDTH)
        x = x + y @ w_out[l]
        mem_n = rmsnorm(mem, norm_mem_g[l])
        x = x + cross_attention(rmsnorm(x, norm_xattn_g[l]), mem_n, w_xq[l], w_xkv[l], w_xo[l])
        hf = rmsnorm(x, norm_ffn_g[l]) @ w_gate_up[l]
        g, up = jnp.split(hf, 2, axis=-1)
        x = x + (jax.nn.silu(g) * up) @ w_down[l]
    return rmsnorm(x, final_norm_g)


_drawn_inputs = setup_inputs


def setup_inputs(seed=0):
    import zlib

    import numpy as np

    out = dict(_drawn_inputs(seed))
    spreads = {}
    factors = {'swa_sinks': 8.0,
     'conv_ln_g': 4.469,
     'conv_ln_b': 4.852,
     'group_norm_g': 2.741,
     'norm_xattn_g': 8.0,
     'norm_mem_g': 8.0,
     'norm_ffn_g': 3.855,
     'final_norm_g': 2.877}
    for name, (base, spread) in spreads.items():
        noise = np.random.default_rng([zlib.crc32(name.encode()), seed]).standard_normal(out[name].shape)
        drawn = base * np.exp(spread * noise) if base else spread * noise
        out[name] = __import__('jax').numpy.asarray(drawn.astype(out[name].dtype))
    for name, factor in factors.items():
        out[name] = (out[name] * factor).astype(out[name].dtype)
    return out
```

```python
from contextlib import ExitStack

import numpy as np

import concourse.bass as bass
from concourse import mybir

F32, F32R, I32 = mybir.dt.float32, mybir.dt.float32r, mybir.dt.int32
ALU = mybir.AluOpType
ACT = mybir.ActivationFunctionType
AX_X = mybir.AxisListType.X

P = 128
D_MODEL, SEQ, DEPTH, N_MEM = 2048, 256, 2, 256
KT = D_MODEL // P
GROUP = 512
GT = GROUP // P
HD = 64
SB_HD = 128
CONV_WIDTH = 31
PADW = CONV_WIDTH - 1
D_FF = 5632
FF_CHUNKS = 2
FT = D_FF // P // FF_CHUNKS
MAX_REL = 128
N_REL = 2 * MAX_REL + 1
NEG = -1e30
EPS = 1e-6
LN2PI = 2 * np.pi

T_MK, T_PW, T_MV, T_OUT, T_XQ, T_XO, T_FF = 38, 42, 46, 50, 66, 70, 86
FF_TILES = 2 * FT + KT
TILES = T_FF + FF_CHUNKS * FF_TILES
PIECE = 8
RING = 4
Q_PW, Q_MV, Q_OUT, Q_XQ, Q_XO, Q_FF = 84, 88, 96, 128, 136, 152
DN_PIECES = (8, 8, FT - 16)
FF_PIECES = 4 * FT + 3 * KT
PIECES = Q_FF + FF_CHUNKS * FF_PIECES
assert PIECES % RING == 0 and FF_PIECES % RING == 0 and TILES % 2 == 0

C_XG, C_MG, C_FG, C_AG, C_GG, C_DW = 0, 16, 32, 48, 64, 80
C_DB = C_DW + GT * CONV_WIDTH
C_LG, C_LB, C_PB, C_SK = C_DB + 4, C_DB + 8, C_DB + 12, C_DB + 16
NPAR = C_SK + 16
K_ID, K_TRI, K_ONE, K_ROT, K_MSK, K_INV = 0, 128, 256, 384, 512, 640
K_G0, K_GF = 641, 641 + KT
NCONST = K_GF + KT

U_QA, U_KA, U_VA, U_QC, U_KC, U_VC, U_QB, U_KB, U_VB = 0, 4, 8, 12, 16, 20, 24, 28, 29
U_TILES = 30
U_MEM = 12

NX = 4
N_U = 46
N_S = 16
N_P = 12
N_STAT = 10
ST_X1, ST_MEM, ST_MU, ST_VAR, ST_A, ST_B, ST_C, ST_D, ST_X2, ST_X3 = range(N_STAT)
N_X = 3 * KT

H_VA, H_A = 20, 20
H_ROPE, H_VB, H_B = 26, 28, 29
H_VC, H_C = 38, 38
H_STAT = {0: ST_X1, 12: ST_MEM, 34: ST_MU, 36: ST_VAR, 37: ST_A, 39: ST_B, 45: ST_C, 48: ST_D}
H_Z = 37
PAIRS = [("B", j) for j in range(4)] + [("C", j) for j in range(4)]
ROPE_TILES = [(H_ROPE, 0), (H_ROPE, 1), (H_ROPE + 1, 2), (H_ROPE + 1, 3), (H_ROPE + 2, 4)]
SPLITS = {37: (ST_A, 0), 39: (ST_B, 1), 45: (ST_C, 2), 48: (ST_D, 3)}


def win_dest(i):
    if i < 8:
        return ("gate", "value")[i % 2], i // 2
    if i < 20:
        return "u", i - 8
    if i < 26:
        return "u", U_QB + i - 20
    return "u", U_QC + i - 26


def u_count(i):
    if i < 8:
        return i // 2 + 1
    if i < T_PW:
        return i - 8 + 5
    if i < T_OUT:
        return i - T_MV + 39
    return i - T_XQ + 43


def tile_pieces(i):
    if T_PW <= i < T_MV:
        return [(Q_PW + i - T_PW, 0, 4)]
    if T_XO <= i < T_FF:
        return [(Q_XO + i - T_XO, 0, 4)]
    if i == T_FF:
        q = Q_FF
    elif i >= T_XQ:
        q = Q_XQ + 2 * (i - T_XQ)
    elif i >= T_OUT:
        q = Q_OUT + 2 * (i - T_OUT)
    elif i >= T_MV:
        q = Q_MV + 2 * (i - T_MV)
    else:
        q = 2 * i
    return [(q, 0, 8), (q + 1, 8, 8)]


def pair_at(t, lag):
    t -= lag
    if H_B <= t < H_B + 4:
        return t - H_B
    if H_C <= t < H_C + 4:
        return 4 + t - H_C
    return None


def head_at(t, lag):
    return t - lag - H_A if H_A <= t - lag < H_A + 4 else None


SCALE_A, SCALE_B = float(SB_HD) ** -0.5, float(HD) ** -0.5
ROUND = 12582912.0
TWO_PI_1 = 6.28125
TWO_PI_2 = float(np.float32(round((2 * np.pi - TWO_PI_1) * 2 ** 20) / 2 ** 20))
TWO_PI_3 = float(np.float32(2 * np.pi - TWO_PI_1 - TWO_PI_2))
PI_IN = 3.1415925
POOL_LINKS, POOL_START = 400, 31
ACT_LINKS, DVE_LINKS, DVE_START = 27, 149, 17


def build(nc, a):
    ctx = ExitStack()
    with ctx:
        def sb(name, shape, dt=F32):
            return ctx.enter_context(nc.sbuf_tensor(name, shape, dt))

        def sem(name):
            return ctx.enter_context(nc.semaphore(name))

        x = sb("x", [P, KT, SEQ])
        act_a = sb("act_a", [P, KT, 2 * SEQ], F32R)
        act_h = sb("act_h", [P, FT, 2 * SEQ], F32R)
        u = sb("u", [P, U_TILES, SEQ])
        raw = sb("raw", [P, RING, PIECE * P])
        w_hi = sb("w_hi", [P, RING, PIECE * P], F32R)
        w_lo = sb("w_lo", [P, RING, PIECE * P], F32R)
        hpad = sb("hpad", [P, GT, PADW + SEQ])
        conv = sb("conv", [P, GT, SEQ])
        prob = sb("prob", [P, 2, 2, 384])
        probt = sb("probt", [P, 2, 384])
        bias = sb("bias", [P, 2, 2, 2 * P])
        cos = sb("cos", [P, SEQ])
        sin = sb("sin", [P, SEQ])
        small = sb("small", [P, 2, SEQ])
        ev = sb("ev", [P, 2, SEQ])
        rx = sb("rx", [P, SEQ])
        rmem = sb("rmem", [P, SEQ])
        rg = sb("rg", [P, SEQ])
        acc = sb("acc", [P, SEQ])
        sq = sb("sq", [P, SEQ])
        par = sb("par", [P, NPAR])
        const = sb("const", [P, NCONST])
        eps = sb("eps", [P, 1])
        nmax = sb("nmax", [P, 2, 4])
        total = sb("total", [P, 2, 4])
        esink = sb("esink", [P, 2, 4])

        ps = ctx.enter_context(nc.psum_tensor("ps", [P, 8, 512], F32))
        gemm = [ps[:, 0, :], ps[:, 1, :]]
        stat = ps[:, 2, 0:SEQ]
        score = [ps[:, 3, :], ps[:, 4, :]]
        turn = [ps[:, 5, :], ps[:, 6, :]]
        pv = ps[:, 7, 0:SEQ]

        ident = const[:, K_ID:K_ID + P]
        tri = const[:, K_TRI:K_TRI + P]
        ones = const[:, K_ONE:K_ONE + P]
        rot = const[:, K_ROT:K_ROT + P]
        mask = const[:, K_MSK:K_MSK + P]

        def flat(ap):
            return ap.rearrange("p k t -> p (k t)")

        vtok = {"A": flat(u[:, U_VA:U_VA + 4, :]), "C": flat(u[:, U_VC:U_VC + 4, :]),
                "B": u[:, U_VB, :], "X": flat(u[:, U_VA:U_VA + 4, :])}
        prob_x = [flat(prob[:, q, :, :])[:, 0:512] for q in range(2)]
        probt_x = flat(probt[:, :, :])[:, 0:512]
        group_out = {0: [u[:, U_QA + k, :] for k in range(GT)], 1: [u[:, U_QB + k, :] for k in range(GT)],
                     2: [u[:, U_QC + k, :] for k in range(GT)], 3: [conv[:, k, :] for k in range(GT)]}

        def pair_tiles(p):
            g, j = PAIRS[p]
            if g == "B":
                return U_QB + j, U_KB, [vtok["B"][:, t * P:(t + 1) * P] for t in range(2)], 0
            return (U_QC + j, U_KC + j,
                    [vtok["C"][:, t * 512 + j * P:t * 512 + (j + 1) * P] for t in range(2)], (j + 1) % 2)

        def gain(c):
            return par[:, c:c + 1]

        raw_in = [sem(f"raw_in{b}") for b in range(RING)]
        hi_ready = sem("hi_ready")
        lo_ready = sem("lo_ready")
        piece_done = sem("piece_done")
        t_ready = sem("t_ready")
        evac_done = sem("evac_done")
        const_in, x_in, par_in, mem_in = sem("const_in"), sem("x_in"), sem("par_in"), sem("mem_in")
        bias_in = [sem("bias_in0"), sem("bias_in1")]
        out_in = sem("out_in")
        dve_seq, act_seq, pool_seq = sem("dve_seq"), sem("act_seq"), sem("pool_seq")
        par_free_a, par_free_d = sem("par_free_a"), sem("par_free_d")
        u_ready = sem("u_ready")
        gate_in, gate_out = sem("gate_in"), sem("gate_out")
        trig_in, trig_out = sem("trig_in"), sem("trig_out")
        x_ready = sem("x_ready")
        xh_ready = sem("xh_ready")
        xg_ready = sem("xg_ready")
        mh_ready, mg_ready = sem("mh_ready"), sem("mg_ready")
        sq_ready = sem("sq_ready")
        st_done = sem("st_done")
        ln_ready = sem("ln_ready")
        r_ready = sem("r_ready")
        z_in, z_out = sem("z_in"), sem("z_out")
        zh_ready, z_ready = sem("zh_ready"), sem("z_ready")
        yd_ready = sem("yd_ready")
        vt_done, vt_ready = sem("vt_done"), sem("vt_ready")
        s_done = sem("s_done")
        sp_ready = sem("sp_ready")
        l1_ready = sem("l1_ready")
        sfx_done = sem("sfx_done")
        lw_ready, we_ready, w_ready = sem("lw_ready"), sem("we_ready"), sem("w_ready")
        rot_done, rope_ready = sem("rot_done"), sem("rope_ready")
        nm_ready = sem("nm_ready")
        e_ready = sem("e_ready")
        p_ready = sem("p_ready")
        tr_done, pt_ready = sem("tr_done"), sem("pt_ready")
        pv_done, y_ready = sem("pv_done"), sem("y_ready")
        yn_ready, yh_ready, yg_ready = sem("yn_ready"), sem("yh_ready"), sem("yg_ready")
        oh_ready, o_ready = sem("oh_ready"), sem("o_ready")
        gs_ready, sil_ready = sem("gs_ready"), sem("sil_ready")
        prod_ready, hh_ready, h_ready = sem("prod_ready"), sem("hh_ready"), sem("h_ready")

        block = ctx.enter_context(nc.Block())

        @block.sync
        def _(sp):
            sp.dma_start(x[:, 0:4, :], a["x"][:, 0:4, :]).then_inc(x_in, 16)
            sp.dma_start(const[:, :], a["const"]).then_inc(const_in, 16)
            for h in range(1, 4):
                sp.dma_start(x[:, 4 * h:4 * h + 4, :], a["x"][:, 4 * h:4 * h + 4, :]).then_inc(x_in, 16)
            sp.dma_start(cos[:, :].bitcast(I32), a["pos"]).then_inc(const_in, 16)

            with sp.Fori(0, DEPTH) as l:
                base = l * PIECES

                def piece(start, k, blocks, src):
                    sp.wait_ge(lo_ready, start + (k + 1))
                    sp.dma_start(raw[:, k % RING, 0:blocks * P], src).then_inc(raw_in[k % RING], 16)

                def pair_bias(buf, src, used):
                    sp.wait_ge(nm_ready, l * N_P + used)
                    sp.dma_start(bias[:, buf, :, :], src).then_inc(bias_in[buf], 16)

                for i in range(T_OUT):
                    if i == H_B - 2:
                        pair_bias(0, a["win_mask"], 0)
                        pair_bias(1, a["bias"][l, 0], 0)
                    if i == H_C - 2:
                        pair_bias(0, a["bias"][l, 1], 4)
                    if i == H_C + 4:
                        pair_bias(1, a["bias"][l, 2], 5)
                    if i == H_C + 5:
                        pair_bias(0, a["bias"][l, 3], 6)
                    for n, b0, nb in tile_pieces(i):
                        if T_PW <= i < T_MV:
                            src = a["w_pw"][l, i - T_PW]
                        else:
                            src = a["w_main"][l, i if i < T_PW else i - 4][:, b0 * P:(b0 + nb) * P]
                        piece(base, n, nb, src)
                with sp.Fori(0, KT // 2) as j:
                    for k in range(4):
                        piece(base + j * 4 + Q_OUT, k, 8,
                              a["w_out"][l, j * 2 + k // 2][:, (k % 2) * 8 * P:(k % 2 + 1) * 8 * P])
                for k in range(8):
                    piece(base + Q_XQ, k, 8, a["w_xq"][l, k // 2][:, (k % 2) * 8 * P:(k % 2 + 1) * 8 * P])
                with sp.Fori(0, KT // 4) as j:
                    for k in range(4):
                        piece(base + j * 4 + Q_XO, k, 4, a["w_xo"][l, j * 4 + k])
                with sp.Fori(0, FF_CHUNKS) as c:
                    gate = base + c * FF_PIECES + Q_FF
                    down = base + c * FF_PIECES + (Q_FF + 4 * FT)
                    with sp.Fori(0, FT) as j:
                        for k in range(4):
                            piece(gate + j * 4, k, 8,
                                  a["w_gu"][l, c, j * 2 + k // 2][:, (k % 2) * 8 * P:(k % 2 + 1) * 8 * P])
                    with sp.Fori(0, KT // 4) as j:
                        for k in range(12):
                            b0, nb = 8 * (k % 3), DN_PIECES[k % 3]
                            piece(down + j * 12, k, nb, a["w_dn"][l, c, j * 4 + k // 3][:, b0 * P:(b0 + nb) * P])
            for h in range(4):
                sp.wait_ge(x_ready, DEPTH * N_X + 4 * h + 4)
                sp.dma_start(a["out"][:, 4 * h:4 * h + 4, :], x[:, 4 * h:4 * h + 4, :]).then_inc(out_in, 16)
            sp.wait_ge(out_in, 64)

        @block.gpsimd
        def _(pool):
            seq = [0]

            def link(ins, base):
                seq[0] += 1
                ins.then_inc(pool_seq, 1)
                pool.wait_ge(pool_seq, base + seq[0])

            def square_sum(srcs, base, wait):
                for k, s in enumerate(srcs):
                    wait(k)
                    if k == 0:
                        link(nc.gpsimd.tensor_tensor(acc[:, :], s, s, ALU.mult), base)
                        continue
                    link(nc.gpsimd.tensor_tensor(sq[:, :], s, s, ALU.mult), base)
                    ins = nc.gpsimd.tensor_tensor(acc[:, :], acc[:, :], sq[:, :], ALU.add)
                    if k == len(srcs) - 1:
                        ins.then_inc(sq_ready, 1)
                    else:
                        link(ins, base)

            link(nc.gpsimd.memset(hpad[:, :, 0:PADW], 0.0), 0)
            square_sum([x[:, k, :] for k in range(KT)], 0,
                       lambda k: pool.wait_ge(x_in, 64) if k == 0 else None)
            assert seq[0] == POOL_START, seq[0]
            seq[0] = 0
            with pool.Fori(0, DEPTH) as l:
                base = l * POOL_LINKS + POOL_START

                def along(column):
                    return column.broadcast_to([P, SEQ])

                def used_up(n):
                    pool.wait_ge(r_ready, l * N_STAT + n)

                pool.wait_ge(par_free_a, l)
                pool.wait_ge(par_free_d, l)
                pool.dma_start(par[:, :], a["par"][l]).then_inc(par_in, 16)
                pool.dma_start(u[:, U_MEM:U_MEM + KT, :], a["mem"]).then_inc(mem_in, 16)
                pool.wait_ge(mem_in, l * 16 + 16)
                used_up(ST_MEM)
                square_sum([u[:, U_MEM + k, :] for k in range(KT)], base, lambda k: None)
                pool.wait_ge(par_in, l * 16 + 16)
                for j in range(GT):
                    pool.wait_ge(u_ready, l * N_U + u_count(2 * j + 1))
                    for tap in range(CONV_WIDTH):
                        src = hpad[:, j, tap:tap + SEQ]
                        w = gain(C_DW + j * CONV_WIDTH + tap)
                        if tap == 0:
                            link(nc.gpsimd.tensor_tensor(conv[:, j, :], src, along(w), ALU.mult), base)
                            link(nc.gpsimd.tensor_tensor(conv[:, j, :], conv[:, j, :], along(gain(C_DB + j)), ALU.add), base)
                            continue
                        link(nc.gpsimd.tensor_tensor(sq[:, :], src, along(w), ALU.mult), base)
                        link(nc.gpsimd.tensor_tensor(conv[:, j, :], conv[:, j, :], sq[:, :], ALU.add), base)
                used_up(ST_MU)
                link(nc.gpsimd.tensor_tensor(acc[:, :], conv[:, 0, :], conv[:, 1, :], ALU.add), base)
                link(nc.gpsimd.tensor_tensor(acc[:, :], acc[:, :], conv[:, 2, :], ALU.add), base)
                nc.gpsimd.tensor_tensor(acc[:, :], acc[:, :], conv[:, 3, :], ALU.add).then_inc(sq_ready, 1)
                used_up(ST_VAR)
                square_sum(group_out[3], base, lambda k: None)
                for n, g in ((ST_A, 0), (ST_B, 1), (ST_C, 2)):
                    used_up(n)
                    square_sum(group_out[g], base,
                               lambda k, g=g: pool.wait_ge(y_ready, l * 12 + 4 * g + k + 1))
                used_up(ST_D)
                square_sum(group_out[3], base, lambda k: pool.wait_ge(yd_ready, l * GT + k + 1))
                for n in range(3):
                    used_up(ST_X2 + n)
                    square_sum([x[:, k, :] for k in range(KT)], base,
                               lambda k, n=n: pool.wait_ge(x_ready, l * N_X + n * KT + k + 1))
            assert seq[0] == POOL_LINKS, seq[0]

        @block.scalar
        def _(act):
            seq = [0]

            def link(ins, base):
                seq[0] += 1
                ins.then_inc(act_seq, 1)
                act.wait_ge(act_seq, base + seq[0])

            def high(start, k, blocks):
                b = k % RING
                act.wait_ge(raw_in[b], start * (16 // RING) + (16 * (k // RING) + 16))
                act.wait_ge(piece_done, start + (k + 1))
                nc.scalar.activation(w_hi[:, b, 0:blocks * P], raw[:, b, 0:blocks * P], ACT.Copy)\
                  .then_inc(hi_ready, 1)

            def small_out(i, last, b=None):
                act.wait_ge(piece_done, last + (RING + 1))
                src, dst = gemm[i % 2][:, SEQ:2 * SEQ], small[:, i % 2, :]
                if b is None:
                    nc.scalar.activation(dst, src, ACT.Copy).then_inc(t_ready, 1)
                else:
                    nc.scalar.activation(dst, src, ACT.Identity, bias=b).then_inc(t_ready, 1)

            def guess(l, n, lbase):
                width = D_MODEL if n in (ST_X1, ST_MEM, ST_X2, ST_X3) else GROUP
                dst = {ST_X1: rx, ST_X2: rx, ST_X3: rx, ST_MEM: rmem}.get(n, rg)
                act.wait_ge(st_done, l * N_STAT + (n + 1))
                link(nc.scalar.activation(acc[:, :], stat, ACT.Identity, bias=eps[:, 0:1], scale=1.0 / width), lbase)
                link(nc.scalar.activation(dst[:, :], acc[:, :], ACT.Ln), lbase)
                nc.scalar.activation(dst[:, :], dst[:, :], ACT.Exp, scale=-0.5).then_inc(ln_ready, 1)

            act.wait_ge(trig_in, 2)
            nc.scalar.activation(cos[:, :], cos[:, :], ACT.Sin).then_inc(trig_out, 1)
            nc.scalar.activation(sin[:, :], sin[:, :], ACT.Sin).then_inc(trig_out, 1)
            for k in range(KT):
                if k % 4 == 0:
                    act.wait_ge(x_in, 64)
                nc.scalar.activation(act_a[:, k, 0:SEQ], x[:, k, :], ACT.Identity,
                                     scale=const[:, K_G0 + k:K_G0 + k + 1]).then_inc(xh_ready, 1)

            with act.Fori(0, DEPTH) as l:
                base = l * PIECES
                lbase = l * ACT_LINKS
                for n, _, nb in tile_pieces(0):
                    high(base, n, nb)
                act.wait_ge(par_in, l * 16 + 16)
                act.wait_ge(mem_in, l * 16 + 16)

                def values_out(which, n):
                    act.wait_ge(vt_done, l * 4 + n)
                    v = vtok[which]
                    if which == "B":
                        nc.scalar.activation(v, turn[1][:, 0:2 * P], ACT.Copy).then_inc(vt_ready, 1)
                    else:
                        nc.scalar.activation(v[:, 0:512], turn[0], ACT.Copy)
                        nc.scalar.activation(v[:, 512:1024], turn[1], ACT.Copy).then_inc(vt_ready, 1)

                def exp_pair(p):
                    q = p % 2
                    act.wait_ge(nm_ready, l * N_P + p + 1)
                    if PAIRS[p][0] == "B":
                        nc.scalar.activation(esink[:, q, :], esink[:, q, :], ACT.Exp)
                    for c in range(4):
                        s = prob[:, q, c % 2, 0:256] if c < 2 else prob[:, q, c % 2, 256:384]
                        ins = nc.scalar.activation(s, s, ACT.Exp, bias=nmax[:, q, c:c + 1],
                                                   accum_out=total[:, q, c:c + 1])
                    ins.then_inc(e_ready, 1)

                def attention_out(dst, n):
                    act.wait_ge(pv_done, l * N_S + n + 1)
                    nc.scalar.activation(dst, pv, ACT.Copy).then_inc(y_ready, 1)

                for i in range(T_OUT):
                    for n, _, nb in tile_pieces(i + 1):
                        high(base, n, nb)
                    if i - 1 in SPLITS:
                        g = SPLITS[i - 1][1]
                        for k in range(GT):
                            act.wait_ge(yn_ready, l * KT + GT * g + k + 1)
                            nc.scalar.activation(act_a[:, GT * g + k, 0:SEQ], group_out[g][k], ACT.Copy)\
                              .then_inc(yh_ready, 1)
                    if i - 1 == H_Z:
                        act.wait_ge(z_in, l + 1)
                        for k in range(GT):
                            ins = nc.scalar.activation(conv[:, k, :], conv[:, k, :], ACT.Silu,
                                                       bias=gain(C_LB + k), scale=gain(C_LG + k))
                        link(ins, lbase)
                        for k in range(GT):
                            nc.scalar.activation(act_h[:, KT + k, 0:SEQ], conv[:, k, :], ACT.Copy).then_inc(zh_ready, 1)
                    small_out(i, base + tile_pieces(i)[-1][0], gain(C_PB + i - T_PW) if T_PW <= i < T_MV else None)
                    if i in H_STAT and H_STAT[i] != ST_MU:
                        guess(l, H_STAT[i], lbase)
                    if i < 8 and i % 2 == 0:
                        act.wait_ge(gate_in, l * GT + i // 2 + 1)
                        nc.scalar.activation(conv[:, i // 2, :], conv[:, i // 2, :], ACT.Sigmoid).then_inc(gate_out, 1)
                    if 2 <= i < 2 + KT:
                        k = i - 2
                        nc.scalar.activation(act_h[:, k, 0:SEQ], u[:, U_MEM + k, :], ACT.Identity,
                                             scale=gain(C_MG + k)).then_inc(mh_ready, 1)
                    h = head_at(i, 2)
                    if h is not None:
                        attention_out(u[:, U_QA + h, :], h)
                    h = head_at(i, 1)
                    if h is not None:
                        act.wait_ge(lw_ready, l * 4 + h + 1)
                        nc.scalar.activation(prob[:, h % 2, 0, :], prob[:, h % 2, 0, :], ACT.Exp).then_inc(we_ready, 1)
                    if i == H_VA:
                        values_out("A", 1)
                    h = head_at(i, 0)
                    if h is not None:
                        z = prob[:, h % 2, 0, :]
                        act.wait_ge(s_done, l * N_S + h + 1)
                        link(nc.scalar.activation(z, score[h % 2][:, 0:384], ACT.Abs, scale=SCALE_A), lbase)
                        link(nc.scalar.activation(z, z, ACT.Exp, scale=-1.0), lbase)
                        nc.scalar.activation(z, z, ACT.Ln, bias=1.0).then_inc(sp_ready, 1)
                    p = pair_at(i, 2)
                    if p is not None:
                        attention_out(u[:, pair_tiles(p)[0], :], 4 + p)
                    if i == H_VB:
                        values_out("B", 2)
                    if i == H_VC:
                        values_out("C", 3)
                    p = pair_at(i, 1)
                    if p is not None:
                        act.wait_ge(tr_done, l * N_P + p + 1)
                        nc.scalar.activation(probt[:, 0, :], turn[0][:, 0:384], ACT.Copy)
                        nc.scalar.activation(probt[:, 1, :], turn[1][:, 0:384], ACT.Copy).then_inc(pt_ready, 1)
                    p = pair_at(i, 0)
                    if p is not None:
                        exp_pair(p)

                def residual_high(j, n, dst, g):
                    act.wait_ge(x_ready, l * N_X + n * KT + j + 1)
                    nc.scalar.activation(dst[:, j, 0:SEQ], x[:, j, :], ACT.Identity,
                                         scale=gain(g + j)).then_inc(xh_ready, 1)

                for i in range(T_OUT, T_XO):
                    for n, _, nb in tile_pieces(i + 1):
                        high(base, n, nb)
                    small_out(i, base + tile_pieces(i)[-1][0])
                    if i < T_XQ:
                        residual_high(i - T_OUT, 0, act_h, C_XG)
                    if i == T_XQ:
                        guess(l, ST_X2, lbase)

                def x_exp(h):
                    q = h % 2
                    act.wait_ge(nm_ready, l * N_P + 8 + h + 1)
                    for t in range(2):
                        v = slice(t * 256, t * 256 + 256)
                        ins = nc.scalar.activation(prob_x[q][:, v], score[q][:, v], ACT.Exp, bias=nmax[:, q, t:t + 1],
                                                   scale=SCALE_A, accum_out=total[:, q, t:t + 1])
                    ins.then_inc(e_ready, 1)

                values_out("X", 4)
                x_exp(0)
                x_exp(1)
                for h in range(NX):
                    act.wait_ge(tr_done, l * N_P + 8 + h + 1)
                    nc.scalar.activation(probt_x, turn[h % 2], ACT.Copy).then_inc(pt_ready, 1)
                    if h + 2 < NX:
                        x_exp(h + 2)
                    act.wait_ge(pv_done, l * N_S + 12 + h + 1)
                    nc.scalar.activation(act_h[:, h, 0:SEQ], pv, ACT.Copy).then_inc(oh_ready, 1)

                for i in range(T_XO, T_FF):
                    for n, _, nb in tile_pieces(i + 1):
                        high(base, n, nb)
                    small_out(i, base + tile_pieces(i)[-1][0])
                    residual_high(i - T_XO, 1, act_a, C_FG)

                for c in range(FF_CHUNKS):
                    gate, down = base + (Q_FF + c * FF_PIECES), base + (Q_FF + c * FF_PIECES + 4 * FT)

                    def quad(j, first=False, end=False):
                        at = gate + j * 4
                        for s in range(4):
                            for k in (2 * s + 2, 2 * s + 3):
                                high(at, k, 8)
                            small_out(s, at + (2 * s + 1))
                            if first and s == 0:
                                guess(l, ST_X3, lbase)
                            n, q = l * (FF_CHUNKS * FT) + j + (c * FT + s // 2 + 1), s // 2
                            if s % 2 == 0:
                                act.wait_ge(gs_ready, n)
                                nc.scalar.activation(conv[:, q, :], conv[:, q, :], ACT.Silu).then_inc(sil_ready, 1)
                            else:
                                act.wait_ge(prod_ready, n)
                                nc.scalar.activation(act_h[:, j + q, 0:SEQ], conv[:, 2 + q, :], ACT.Copy).then_inc(hh_ready, 1)

                    quad(0, first=c == 0)
                    with act.Fori(1, FT // 2) as jq:
                        quad(jq * 2)
                    for j in range(KT):
                        high(down, 3 * j + 2, DN_PIECES[2])
                        if j + 1 < KT or c + 1 < FF_CHUNKS:
                            for k in range(2):
                                high(down, 3 * j + 3 + k, 8)
                        small_out(j, down + (3 * j + 2))
                        if c == FF_CHUNKS - 1:
                            residual_high(j, 2, act_a, C_AG)
                nc.scalar.activation(eps[:, 0:1], eps[:, 0:1], ACT.Copy).then_inc(par_free_a, 1)
            assert seq[0] == ACT_LINKS, seq[0]
            act.wait_ge(par_free_a, DEPTH)
            guess(DEPTH, ST_X1, DEPTH * ACT_LINKS - ACT_LINKS)

        @block.vector
        def _(dve):
            V = nc.vector
            seq = [0]

            def link(ins, base):
                seq[0] += 1
                ins.then_inc(dve_seq, 1)
                dve.wait_ge(dve_seq, base + seq[0])

            def low(start, k, blocks):
                b = k % RING
                dve.wait_ge(hi_ready, start + (k + 1))
                V.tensor_tensor(w_lo[:, b, 0:blocks * P], raw[:, b, 0:blocks * P],
                                w_hi[:, b, 0:blocks * P].bitcast(F32), ALU.subtract).then_inc(lo_ready, 1)

            def add_products(i, number, dst=None):
                dve.wait_ge(t_ready, number + 1)
                V.tensor_tensor(ev[:, i % 2, :], gemm[i % 2][:, 0:SEQ], small[:, i % 2, :], ALU.add)\
                 .then_inc(evac_done, 1)
                dve.wait_ge(evac_done, number + 3)
                return ev[:, i % 2, :]

            def refine(l, n, lbase, i, final=True):
                dst = {ST_X1: rx, ST_X2: rx, ST_X3: rx, ST_MEM: rmem}.get(n, rg)[:, :]
                tmp = ev[:, (i + 1) % 2, :]
                dve.wait_ge(ln_ready, l * (N_STAT - 1) + (n + 1 if n < ST_MU else n))
                link(V.tensor_tensor(tmp, dst, dst, ALU.mult), lbase)
                link(V.scalar_tensor_tensor(out=tmp, in0=tmp, scalar=-0.5, in1=acc[:, :], op0=ALU.mult, op1=ALU.mult), lbase)
                ins = V.scalar_tensor_tensor(out=dst, in0=tmp, scalar=1.5, in1=dst, op0=ALU.add, op1=ALU.mult)
                if final:
                    ins.then_inc(r_ready, 1)
                    dve.wait_ge(r_ready, l * N_STAT + (n + 1))
                else:
                    link(ins, lbase)

            V.memset(ev[:, 0, :], 0.0).then_inc(lo_ready, RING)
            V.memset(ev[:, 1, :], 0.0).then_inc(piece_done, RING)
            V.memset(esink[:, :, :], 0.0).then_inc(evac_done, 2)
            link(V.memset(eps[:, :], EPS), 0)
            dve.wait_ge(const_in, 32)
            link(V.tensor_copy(sin[:, :], cos[:, :].bitcast(I32)), 0)
            link(V.tensor_scalar(sin[:, :], sin[:, :], const[:, K_INV:K_INV + 1], None, ALU.mult), 0)
            for dst, turns, shift in ((cos, 0.25, np.pi / 2), (sin, 0.0, 0.0)):
                n = ev[:, 0, :]
                link(V.tensor_scalar(n, sin[:, :], 1.0 / (2 * np.pi), turns, ALU.mult, ALU.add), 0)
                link(V.tensor_scalar(n, n, ROUND, None, ALU.add), 0)
                link(V.tensor_scalar(n, n, ROUND, None, ALU.subtract), 0)
                link(V.scalar_tensor_tensor(out=dst[:, :], in0=n, scalar=-TWO_PI_1, in1=sin[:, :], op0=ALU.mult, op1=ALU.add), 0)
                link(V.scalar_tensor_tensor(out=dst[:, :], in0=n, scalar=-TWO_PI_2, in1=dst[:, :], op0=ALU.mult, op1=ALU.add), 0)
                link(V.scalar_tensor_tensor(out=dst[:, :], in0=n, scalar=-TWO_PI_3, in1=dst[:, :], op0=ALU.mult, op1=ALU.add), 0)
                link(V.tensor_scalar(dst[:, :], dst[:, :], shift, PI_IN, ALU.add, ALU.min), 0)
                V.tensor_scalar(dst[:, :], dst[:, :], -PI_IN, None, ALU.max).then_inc(trig_in, 1)
            dve.wait_ge(trig_out, 2)
            for k in range(KT):
                dve.wait_ge(xh_ready, k + 1)
                V.scalar_tensor_tensor(out=act_a[:, k, SEQ:2 * SEQ], in0=x[:, k, :],
                                       scalar=const[:, K_G0 + k:K_G0 + k + 1], in1=act_a[:, k, 0:SEQ].bitcast(F32),
                                       op0=ALU.mult, op1=ALU.subtract).then_inc(xg_ready, 1)
            assert seq[0] == DVE_START, seq[0]
            seq[0] = 0

            with dve.Fori(0, DEPTH) as l:
                base = l * PIECES
                tile0 = l * TILES
                lbase = l * DVE_LINKS + DVE_START
                for n, _, nb in tile_pieces(0):
                    low(base, n, nb)
                dve.wait_ge(par_in, l * 16 + 16)
                dve.wait_ge(mem_in, l * 16 + 16)

                def rope(i, k):
                    t, tmp = u[:, U_QB + k, :], ev[:, i % 2, :]
                    dve.wait_ge(rot_done, l * 5 + k + 1)
                    link(V.tensor_tensor(tmp, turn[k % 2][:, 0:SEQ], sin[:, :], ALU.mult), lbase)
                    link(V.tensor_tensor(t, t, cos[:, :], ALU.mult), lbase)
                    V.tensor_tensor(t, t, tmp, ALU.add).then_inc(rope_ready, 1)
                    dve.wait_ge(rope_ready, l * 5 + k + 1)

                def diagonal(ap):
                    v = ap.rearrange("p (b q) -> p b q", q=P)[:, 0:3:2, :]
                    return v, mask[:, None, :].broadcast_to([P, 2, P])

                def log_beta(h):
                    z, sp_, ls, l1 = score[h % 2][:, 0:384], prob[:, h % 2, 0, :], prob[:, h % 2, 1, :], probt[:, h % 2, :]
                    dve.wait_ge(sp_ready, l * 4 + h + 1)
                    link(V.tensor_scalar(ls, z, SCALE_A, 0.0, ALU.mult, ALU.min), lbase)
                    link(V.tensor_tensor(ls, ls, sp_, ALU.subtract), lbase)
                    link(V.scalar_tensor_tensor(out=l1, in0=z, scalar=-SCALE_A, in1=ls, op0=ALU.mult, op1=ALU.add), lbase)
                    d, m = diagonal(l1)
                    V.tensor_tensor(d, d, m, ALU.mult).then_inc(l1_ready, 1)

                def mask_weights(h):
                    d, m = diagonal(prob[:, h % 2, 0, :])
                    dve.wait_ge(we_ready, l * 4 + h + 1)
                    V.tensor_tensor(d, d, m, ALU.mult).then_inc(w_ready, 1)

                def probabilities(p):
                    q = p % 2
                    dve.wait_ge(e_ready, l * N_P + p + 1)
                    if PAIRS[p][0] == "B":
                        link(V.tensor_tensor(total[:, q, :], total[:, q, :], esink[:, q, :], ALU.add), lbase)
                    link(V.reciprocal(total[:, q, :], total[:, q, :]), lbase)
                    for c in range(4):
                        s = prob[:, q, c % 2, 0:256] if c < 2 else prob[:, q, c % 2, 256:384]
                        ins = V.tensor_scalar(s, s, total[:, q, c:c + 1], None, ALU.mult)
                    ins.then_inc(p_ready, 1)

                def masked_scores(p):
                    q = p % 2
                    b = pair_tiles(p)[3]
                    uses = {0: 3, 1: 2}[b]
                    nth = {0: 1, 1: 1, 2: 1, 3: 1, 4: 1, 5: 2, 6: 2, 7: 3}[p]
                    dve.wait_ge(bias_in[b], l * (16 * uses) + 16 * nth)
                    dve.wait_ge(s_done, l * N_S + 4 + p + 1)
                    for hh in range(2):
                        for lo_, hi_, src in ((0, 256, bias[:, b, hh, :]), (256, 384, bias[:, b, hh, P:2 * P])):
                            ins = V.scalar_tensor_tensor(out=prob[:, q, hh, lo_:hi_], in0=score[hh][:, lo_:hi_],
                                                         scalar=SCALE_B, in1=src, op0=ALU.mult, op1=ALU.add)
                    link(ins, lbase)
                    ins = V.tensor_reduce(nmax[:, q, 0:2], prob[:, q, :, 0:256], AX_X, ALU.max, negate=True)
                    ins = V.tensor_reduce(nmax[:, q, 2:4], prob[:, q, :, 256:384], AX_X, ALU.max, negate=True)
                    if PAIRS[p][0] == "B":
                        sink = par[:, C_SK + 4 * p:C_SK + 4 * p + 4]
                        link(ins, lbase)
                        link(V.tensor_scalar(esink[:, q, :], sink, -1.0, None, ALU.mult), lbase)
                        link(V.tensor_tensor(nmax[:, q, :], nmax[:, q, :], esink[:, q, :], ALU.min), lbase)
                        ins = V.tensor_tensor(esink[:, q, :], sink, nmax[:, q, :], ALU.add)
                    ins.then_inc(nm_ready, 1)

                def normalise(g):
                    for k in range(GT):
                        t = group_out[g][k]
                        ins = V.scalar_tensor_tensor(out=t, in0=t, scalar=gain(C_GG + GT * g + k), in1=rg[:, :],
                                                     op0=ALU.mult, op1=ALU.mult)
                        ins.then_inc(yn_ready, 1)
                    dve.wait_ge(yn_ready, l * KT + GT * g + GT)
                    V.memset(nmax[:, 0, 0:1], 0.0).then_inc(r_ready, 1)

                for i in range(T_OUT):
                    for n, _, nb in tile_pieces(i + 1):
                        low(base, n, nb)
                    if 3 <= i < 3 + KT:
                        k = i - 3
                        dve.wait_ge(mh_ready, l * KT + k + 1)
                        V.scalar_tensor_tensor(out=act_h[:, k, SEQ:2 * SEQ], in0=u[:, U_MEM + k, :], scalar=gain(C_MG + k),
                                               in1=act_h[:, k, 0:SEQ].bitcast(F32), op0=ALU.mult,
                                               op1=ALU.subtract).then_inc(mg_ready, 1)
                    for t, k in ROPE_TILES:
                        if i == t + 1:
                            rope(i, k)
                    h = head_at(i, 2)
                    if h is not None:
                        mask_weights(h)
                    h = head_at(i, 1)
                    if h is not None:
                        log_beta(h)
                    p = pair_at(i, 1)
                    if p is not None:
                        probabilities(p)

                    s = add_products(i, tile0 + i)
                    if i in H_STAT and H_STAT[i] not in (ST_MU, ST_VAR):
                        refine(l, H_STAT[i], lbase, i, final=H_STAT[i] in (ST_X1, ST_MEM))
                    if i < T_MK:
                        kind, j = win_dest(i)
                        if kind == "gate":
                            V.tensor_tensor(conv[:, j, :], s, rx[:, :], ALU.mult).then_inc(gate_in, 1)
                        elif kind == "value":
                            link(V.tensor_tensor(s, s, rx[:, :], ALU.mult), lbase)
                            dve.wait_ge(gate_out, l * GT + j + 1)
                            V.tensor_tensor(hpad[:, j, PADW:], s, conv[:, j, :], ALU.mult).then_inc(u_ready, 1)
                        else:
                            V.tensor_tensor(u[:, j, :], s, rx[:, :], ALU.mult).then_inc(u_ready, 1)
                    elif T_PW <= i < T_MV:
                        V.tensor_copy(conv[:, i - T_PW, :], s).then_inc(yd_ready, 1)
                    else:
                        j = U_KA + i - T_MK if i < T_PW else U_VA + i - T_MV
                        V.tensor_tensor(u[:, j, :], s, rmem[:, :], ALU.mult).then_inc(u_ready, 1)
                    if i in H_STAT and H_STAT[i] == ST_MU:
                        dve.wait_ge(st_done, l * N_STAT + ST_MU + 1)
                        for k in range(GT):
                            ins = V.scalar_tensor_tensor(out=conv[:, k, :], in0=stat, scalar=-1.0 / GROUP,
                                                         in1=conv[:, k, :], op0=ALU.mult, op1=ALU.add)
                        ins.then_inc(r_ready, 1)
                    if i in H_STAT and H_STAT[i] == ST_VAR:
                        refine(l, ST_VAR, lbase, i, final=False)
                        for k in range(GT):
                            ins = V.tensor_tensor(conv[:, k, :], conv[:, k, :], rg[:, :], ALU.mult)
                        ins.then_inc(z_in, 1)
                        dve.wait_ge(z_in, l + 1)
                        V.memset(nmax[:, 0, 0:1], 0.0).then_inc(r_ready, 1)
                    if i == H_Z + 2:
                        for k in range(GT):
                            dve.wait_ge(zh_ready, l * GT + k + 1)
                            V.tensor_tensor(act_h[:, KT + k, SEQ:2 * SEQ], conv[:, k, :],
                                            act_h[:, KT + k, 0:SEQ].bitcast(F32), ALU.subtract).then_inc(z_ready, 1)
                    if i in SPLITS:
                        normalise(SPLITS[i][1])
                    if i - 1 in SPLITS:
                        g = SPLITS[i - 1][1]
                        for k in range(GT):
                            dve.wait_ge(yh_ready, l * KT + GT * g + k + 1)
                            V.tensor_tensor(act_a[:, GT * g + k, SEQ:2 * SEQ], group_out[g][k],
                                            act_a[:, GT * g + k, 0:SEQ].bitcast(F32), ALU.subtract).then_inc(yg_ready, 1)
                    h = head_at(i, 1)
                    if h is not None:
                        dve.wait_ge(sfx_done, l * 4 + h + 1)
                        V.tensor_tensor(prob[:, h % 2, 0, :], turn[h % 2][:, 0:384], prob[:, h % 2, 1, :], ALU.add)\
                         .then_inc(lw_ready, 1)
                    p = pair_at(i, 0)
                    if p is not None:
                        masked_scores(p)

                def residual(j, s, number):
                    ins = V.tensor_tensor(x[:, j, :], x[:, j, :], s, ALU.add)
                    if number is None:
                        link(ins, lbase)
                    else:
                        ins.then_inc(x_ready, 1)
                        dve.wait_ge(x_ready, l * N_X + (number * KT + j + 1))

                def residual_low(j, n, dst, g):
                    dve.wait_ge(xh_ready, l * N_X + (KT + n * KT + j + 1))
                    V.scalar_tensor_tensor(out=dst[:, j, SEQ:2 * SEQ], in0=x[:, j, :], scalar=gain(g + j),
                                           in1=dst[:, j, 0:SEQ].bitcast(F32), op0=ALU.mult,
                                           op1=ALU.subtract).then_inc(xg_ready, 1)

                for i in range(T_OUT, T_XO):
                    for n, _, nb in tile_pieces(i + 1):
                        low(base, n, nb)
                    if i < T_XQ:
                        j = i - T_OUT
                        if j:
                            residual_low(j - 1, 0, act_h, C_XG)
                        residual(j, add_products(i, tile0 + i), 0)
                        if j == KT - 1:
                            residual_low(j, 0, act_h, C_XG)
                    else:
                        s = add_products(i, tile0 + i)
                        if i == T_XQ:
                            refine(l, ST_X2, lbase, i)
                        V.tensor_tensor(u[:, U_QC + i - T_XQ, :], s, rx[:, :], ALU.mult).then_inc(u_ready, 1)

                def x_max(h):
                    q = h % 2
                    dve.wait_ge(s_done, l * N_S + 12 + h + 1)
                    link(V.tensor_reduce(nmax[:, q, 0:2], score[q].rearrange("p (t k) -> p t k", t=2), AX_X, ALU.max,
                                         negate=True), lbase)
                    V.tensor_scalar(nmax[:, q, 0:2], nmax[:, q, 0:2], SCALE_A, None, ALU.mult).then_inc(nm_ready, 1)

                def x_prob(h):
                    q = h % 2
                    dve.wait_ge(e_ready, l * N_P + 8 + h + 1)
                    link(V.reciprocal(total[:, q, 0:2], total[:, q, 0:2]), lbase)
                    for t in range(2):
                        s = prob_x[q][:, t * 256:t * 256 + 256]
                        ins = V.tensor_scalar(s, s, total[:, q, t:t + 1], None, ALU.mult)
                    ins.then_inc(p_ready, 1)

                def x_low(h):
                    dve.wait_ge(oh_ready, l * NX + h + 1)
                    V.tensor_tensor(act_h[:, h, SEQ:2 * SEQ], pv, act_h[:, h, 0:SEQ].bitcast(F32), ALU.subtract)\
                     .then_inc(o_ready, 1)

                x_max(0)
                x_max(1)
                for h in range(NX):
                    x_prob(h)
                    if h:
                        x_low(h - 1)
                    if h + 2 < NX:
                        x_max(h + 2)
                x_low(NX - 1)

                for i in range(T_XO, T_FF):
                    for n, _, nb in tile_pieces(i + 1):
                        low(base, n, nb)
                    j = i - T_XO
                    if j:
                        residual_low(j - 1, 1, act_a, C_FG)
                    residual(j, add_products(i, tile0 + i), 1)
                residual_low(KT - 1, 1, act_a, C_FG)

                for c in range(FF_CHUNKS):
                    gate, down = base + (Q_FF + c * FF_PIECES), base + (Q_FF + c * FF_PIECES + 4 * FT)
                    first_tile = T_FF + c * FF_TILES

                    def quad(j, lb, first=False):
                        at = gate + j * 4
                        for s in range(4):
                            for k in (2 * s + 2, 2 * s + 3):
                                low(at, k, 8)
                            e = add_products(s, tile0 + j * 2 + (first_tile + s))
                            if first and s == 0:
                                refine(l, ST_X3, lb, s)
                            n, q = l * (FF_CHUNKS * FT) + j + (c * FT + s // 2 + 1), s // 2
                            if s % 2 == 0:
                                V.tensor_tensor(conv[:, q, :], e, rx[:, :], ALU.mult).then_inc(gs_ready, 1)
                            else:
                                link(V.tensor_tensor(e, e, rx[:, :], ALU.mult), lb)
                                dve.wait_ge(sil_ready, n)
                                V.tensor_tensor(conv[:, 2 + q, :], conv[:, q, :], e, ALU.mult).then_inc(prod_ready, 1)
                                dve.wait_ge(hh_ready, n)
                                V.tensor_tensor(act_h[:, j + q, SEQ:2 * SEQ], conv[:, 2 + q, :],
                                                act_h[:, j + q, 0:SEQ].bitcast(F32), ALU.subtract).then_inc(h_ready, 1)

                    quad(0, lbase, first=c == 0)
                    before = seq[0]
                    with dve.Fori(1, FT // 2) as jq:
                        quad(jq * 2, lbase + jq * 2 - 2)
                    assert seq[0] == before + 2
                    seq[0] = before + 2 * (FT // 2 - 1)
                    for j in range(KT):
                        low(down, 3 * j + 2, DN_PIECES[2])
                        if j + 1 < KT or c + 1 < FF_CHUNKS:
                            for k in range(2):
                                low(down, 3 * j + 3 + k, 8)
                        last_chunk = c == FF_CHUNKS - 1
                        if j and last_chunk:
                            residual_low(j - 1, 2, act_a, C_AG)
                        s = add_products(j, tile0 + (first_tile + 2 * FT + j))
                        residual(j, s, 2 if last_chunk else None)
                residual_low(KT - 1, 2, act_a, C_AG)
                dve.wait_ge(xg_ready, l * N_X + 4 * KT)
                V.memset(nmax[:, 0, 0:1], 0.0).then_inc(par_free_d, 1)
            assert seq[0] == DVE_LINKS, seq[0]
            seq[0] = 0
            refine(DEPTH, ST_X1, DEPTH * DVE_LINKS + DVE_START, 0)
            for k in range(KT):
                V.scalar_tensor_tensor(out=x[:, k, :], in0=x[:, k, :], scalar=const[:, K_GF + k:K_GF + k + 1],
                                       in1=rx[:, :], op0=ALU.mult, op1=ALU.mult).then_inc(x_ready, 1)

        @block.tensor
        def _(pe):
            T = nc.tensor

            def tile(start, number, pieces, rhs, bank, ready=None):
                pe.wait_ge(evac_done, number + 1)
                last = pieces[-1][1] + pieces[-1][2] - 1
                for n, b0, nb in pieces:
                    pe.wait_ge(lo_ready, start + (n + RING + 1))
                    for k in range(nb):
                        kk = b0 + k
                        if ready is not None:
                            ready(kk)
                        w = slice(k * P, (k + 1) * P)
                        if kk < last:
                            T.matmul(bank, w_hi[:, n % RING, w], rhs[:, kk, :], start=kk == 0, stop=False)
                        ins = T.matmul(bank[:, SEQ:2 * SEQ], w_lo[:, n % RING, w], rhs[:, kk, 0:SEQ],
                                       start=False, stop=False)
                        if kk == last:
                            ins = T.matmul(bank, w_hi[:, n % RING, w], rhs[:, kk, :], start=False, stop=True)
                    ins.then_inc(piece_done, 1)

            def statistic(l, n):
                pe.wait_ge(sq_ready, l * N_STAT + (n + 1))
                T.matmul(stat, ones, acc[:, :], start=True, stop=True).then_inc(st_done, 1)

            pe.wait_ge(const_in, 32)
            with pe.Fori(0, DEPTH) as l:
                base, tile0 = l * PIECES, l * TILES

                def turn_values(which, n, ready):
                    pe.wait_ge(u_ready, l * N_U + ready)
                    if which == "B":
                        pe.wait_ge(rope_ready, l * 5 + 4)
                        for t in range(2):
                            ins = T.transpose(turn[1][:, t * P:(t + 1) * P], u[:, U_VB, t * P:(t + 1) * P], ident)
                    else:
                        first = U_VC if which == "C" else U_VA
                        for t in range(2):
                            for j in range(4):
                                ins = T.transpose(turn[t][:, j * P:(j + 1) * P], u[:, first + j, t * P:(t + 1) * P], ident)
                    ins.then_inc(vt_done, 1)

                def head_scores(h):
                    pe.wait_ge(u_ready, l * N_U + u_count(19))
                    q, k = u[:, U_QA + h, :], u[:, U_KA + h, :]
                    T.matmul(score[h % 2][:, 0:256], k[:, 0:P], q, start=True, stop=True)
                    T.matmul(score[h % 2][:, 256:384], k[:, P:2 * P], q[:, P:2 * P], start=False, stop=True,
                             skip_group_check=True).then_inc(s_done, 1)

                def head_suffix(h):
                    l1 = probt[:, h % 2, :]
                    pe.wait_ge(vt_ready, l * 4 + 1)
                    pe.wait_ge(l1_ready, l * 4 + h + 1)
                    T.matmul(turn[h % 2][:, P:2 * P], ones, l1[:, 256:384], start=True, stop=False)
                    T.matmul(turn[h % 2][:, P:2 * P], tri, l1[:, P:2 * P], start=False, stop=True)
                    for v in (slice(0, P), slice(2 * P, 3 * P)):
                        ins = T.matmul(turn[h % 2][:, v], tri, l1[:, v], start=False, stop=True, skip_group_check=True)
                    ins.then_inc(sfx_done, 1)

                def head_output(h):
                    w = prob[:, h % 2, 0, :]
                    pe.wait_ge(w_ready, l * 4 + h + 1)
                    pe.wait_ge(y_ready, l * 12 + h)
                    T.matmul(pv[:, P:2 * P], vtok["A"][:, 512 + h * P:512 + (h + 1) * P], w[:, 256:384],
                             start=True, stop=False)
                    T.matmul(pv[:, P:2 * P], vtok["A"][:, h * P:(h + 1) * P], w[:, P:2 * P], start=False, stop=True)
                    T.matmul(pv[:, 0:P], vtok["A"][:, h * P:(h + 1) * P], w[:, 0:P], start=False, stop=True,
                             skip_group_check=True).then_inc(pv_done, 1)

                def rotate(k):
                    pe.wait_ge(u_ready, l * N_U + u_count(25))
                    if k >= 2:
                        pe.wait_ge(rope_ready, l * 5 + (k - 1))
                    T.matmul(turn[k % 2][:, 0:SEQ], rot, u[:, U_QB + k, :], start=True, stop=True).then_inc(rot_done, 1)

                def pair_scores(p):
                    tq, tk, _, _ = pair_tiles(p)
                    if PAIRS[p][0] == "B":
                        pe.wait_ge(rope_ready, l * 5 + 5)
                    else:
                        pe.wait_ge(u_ready, l * N_U + u_count(37))
                    for hh in range(2):
                        v = slice(64 * hh, 64 * hh + 64)
                        T.matmul(score[hh][:, 0:256], u[v, tq, P:2 * P], u[v, tk, :], start=True, stop=True)
                        ins = T.matmul(score[hh][:, 256:384], u[v, tq, 0:P], u[v, tk, 0:P], start=False, stop=True,
                                       skip_group_check=True)
                    ins.then_inc(s_done, 1)

                def pair_turn(p):
                    pe.wait_ge(vt_ready, l * 4 + (2 if p < 4 else 3))
                    pe.wait_ge(p_ready, l * N_P + p + 1)
                    for hh in range(2):
                        s = prob[:, p % 2, hh, :]
                        T.transpose(turn[hh][:, 0:P], s[:, 256:384], ident)
                        T.transpose(turn[hh][:, P:2 * P], s[:, 0:P], ident)
                        ins = T.transpose(turn[hh][:, 2 * P:3 * P], s[:, P:2 * P], ident)
                    ins.then_inc(tr_done, 1)

                def pair_output(p):
                    _, _, v, _ = pair_tiles(p)
                    pe.wait_ge(pt_ready, l * N_P + p + 1)
                    pe.wait_ge(y_ready, l * 12 + 4 + p)
                    for hh in range(2):
                        rows = slice(64 * hh, 64 * hh + 64)
                        T.matmul(pv[rows, P:2 * P], v[1][:, rows], probt[:, hh, 256:384], start=True, stop=False)
                        T.matmul(pv[rows, P:2 * P], v[0][:, rows], probt[:, hh, P:2 * P], start=False, stop=True)
                        ins = T.matmul(pv[rows, 0:P], v[0][:, rows], probt[:, hh, 0:P], start=False, stop=True,
                                       skip_group_check=True)
                    ins.then_inc(pv_done, 1)

                for i in range(T_OUT):
                    ready, rhs = None, act_a
                    if i == 0:
                        ready = lambda k: pe.wait_ge(xg_ready, l * N_X + k + 1)
                    if i == T_MK:
                        pe.wait_ge(mg_ready, l * KT + KT)
                    if i >= T_MK:
                        rhs = act_h
                    if T_PW <= i < T_MV:
                        rhs = act_h[:, KT:KT + GT, :]
                        if i == T_PW:
                            pe.wait_ge(z_ready, l * GT + GT)
                    tile(base, tile0 + i, tile_pieces(i), rhs, gemm[i % 2], ready)
                    if i in H_STAT:
                        statistic(l, H_STAT[i])
                    h = head_at(i, 2)
                    if h is not None:
                        head_output(h)
                    h = head_at(i, 1)
                    if h is not None:
                        head_suffix(h)
                    if i == H_VA:
                        turn_values("A", 1, u_count(19))
                    h = head_at(i, 0)
                    if h is not None:
                        head_scores(h)
                    for t, k in ROPE_TILES:
                        if i == t:
                            rotate(k)
                    p = pair_at(i, 2)
                    if p is not None:
                        pair_output(p)
                    if i == H_VB:
                        turn_values("B", 2, u_count(25))
                    if i == H_VC:
                        turn_values("C", 3, u_count(37))
                    p = pair_at(i, 1)
                    if p is not None:
                        pair_turn(p)
                    p = pair_at(i, 0)
                    if p is not None:
                        pair_scores(p)

                with pe.Fori(0, KT // 2) as j:
                    for s in range(2):
                        ready = (lambda k: pe.wait_ge(yg_ready, l * KT + (12 if k == 0 else KT)) if k in (0, 12) else None) \
                            if s == 0 else None
                        tile(base + j * 4 + Q_OUT, tile0 + j * 2 + (T_OUT + s), [(2 * s, 0, 8), (2 * s + 1, 8, 8)],
                             act_a, gemm[s], ready)
                for i in range(T_XQ, T_XO):
                    ready = (lambda k: pe.wait_ge(xg_ready, l * N_X + KT + k + 1)) if i == T_XQ else None
                    tile(base, tile0 + i, tile_pieces(i), act_h, gemm[i % 2], ready)
                    if i == T_XQ:
                        statistic(l, ST_X2)

                def x_scores(h):
                    q, k = u[:, U_QC + h, :], u[:, U_KA + h, :]
                    if h < 2:
                        pe.wait_ge(u_ready, l * N_U + u_count(T_XO - 1))
                    for t in range(2):
                        ins = T.matmul(score[h % 2][:, t * 256:t * 256 + 256], q[:, t * P:(t + 1) * P], k,
                                       start=t == 0, stop=True, skip_group_check=True)
                    ins.then_inc(s_done, 1)

                def x_turn(h):
                    pe.wait_ge(p_ready, l * N_P + 8 + h + 1)
                    for k in range(2):
                        for t in range(2):
                            ins = T.transpose(turn[h % 2][:, k * 256 + t * P:k * 256 + (t + 1) * P],
                                              prob_x[h % 2][:, t * 256 + k * P:t * 256 + (k + 1) * P], ident)
                    ins.then_inc(tr_done, 1)

                turn_values("X", 4, u_count(T_OUT - 1))
                x_scores(0)
                x_scores(1)
                pe.wait_ge(vt_ready, l * 4 + 4)
                for h in range(NX):
                    x_turn(h)
                    if h + 2 < NX:
                        x_scores(h + 2)
                    pe.wait_ge(pt_ready, l * N_P + 8 + h + 1)
                    if h:
                        pe.wait_ge(o_ready, l * NX + h)
                    for t in range(2):
                        ins = T.matmul(pv, vtok["X"][:, t * 512 + h * P:t * 512 + (h + 1) * P],
                                       probt_x[:, t * 256:t * 256 + 256], start=t == 0, stop=t == 1)
                    ins.then_inc(pv_done, 1)

                for i in range(T_XO, T_FF):
                    ready = (lambda k: pe.wait_ge(o_ready, l * NX + k + 1)) if i == T_XO else None
                    tile(base, tile0 + i, tile_pieces(i), act_h, gemm[i % 2], ready)

                for c in range(FF_CHUNKS):
                    first_tile, piece0 = T_FF + c * FF_TILES, Q_FF + c * FF_PIECES

                    def quad(j, first=False):
                        for s in range(4):
                            ready = (lambda k: pe.wait_ge(xg_ready, l * N_X + 2 * KT + k + 1)) if first and s == 0 else None
                            tile(base + j * 4 + piece0, tile0 + j * 2 + (first_tile + s),
                                 [(2 * s, 0, 8), (2 * s + 1, 8, 8)], act_a, gemm[s % 2], ready)
                            if first and s == 0:
                                statistic(l, ST_X3)

                    quad(0, first=c == 0)
                    with pe.Fori(1, FT // 2) as jq:
                        quad(jq * 2)
                    with pe.Fori(0, KT // 4) as j:
                        for s in range(4):
                            ready = (lambda k: pe.wait_ge(h_ready, l * (FF_CHUNKS * FT) + (c * FT + (FT - 2 if k == 0 else FT)))
                                     if k in (0, FT - 2) else None) if s == 0 else None
                            tile(base + j * 12 + (piece0 + 4 * FT), tile0 + j * 4 + (first_tile + 2 * FT + s),
                                 [(3 * s + k, 8 * k, DN_PIECES[k]) for k in range(3)], act_h, gemm[s % 2], ready)
            statistic(DEPTH, ST_X1)


def tiles_of(w, cols):
    k = w.shape[0] // P
    w = w.reshape(k, P, w.shape[1])
    out = np.empty((len(cols), P, k, P), w.dtype)
    for n, c in enumerate(cols):
        out[n] = w[:, :, c].transpose(1, 0, 2)
    return out.reshape(len(cols), P, k * P)


def window_heads():
    return [np.r_[j * HD:(j + 1) * HD, (j + 4) * HD:(j + 5) * HD] for j in range(4)]


def win_columns():
    block = lambda at: [np.arange(at + j * P, at + (j + 1) * P) for j in range(4)]
    qa, ka, va, qb, kb, vb, qc, kc, vc, ud = 0, 512, 1024, 1536, 2048, 2176, 2304, 2816, 3328, 3840
    value, gate = block(ud), block(ud + GROUP)
    cols = [t for pair in zip(gate, value) for t in pair]
    cols += block(qa) + block(ka) + block(va)
    cols += [qb + w for w in window_heads()] + [np.arange(kb, kb + P), np.arange(vb, vb + P)]
    return cols + block(qc) + block(kc) + block(vc)


def feature_major(v):
    return np.swapaxes(v.reshape(*v.shape[:-1], -1, P), -1, -2)


def constants():
    c = np.zeros((P, NCONST), np.float32)
    i = np.arange(P)
    c[:, K_ID:K_ID + P] = np.eye(P)
    c[:, K_TRI:K_TRI + P] = i[:, None] > i[None, :]
    c[:, K_ONE:K_ONE + P] = 1.0
    half = HD // 2
    for m in range(P):
        if m % HD < half:
            c[m + half, K_ROT + m] = -1.0
        else:
            c[m - half, K_ROT + m] = 1.0
    c[:, K_MSK:K_MSK + P] = i[:, None] < i[None, :]
    c[:, K_INV] = np.float32(10000.0) ** (-(i % half).astype(np.float32) / np.float32(half))
    return c


def kernel(**inputs):
    import concourse.bacc as bacc
    from concourse.bass_utils import run_bass_kernel_spmd

    v = {k: np.asarray(w) for k, w in inputs.items()}
    L = DEPTH
    heads = window_heads()
    order = np.concatenate([np.arange(GROUP)] + [GROUP + h for h in heads] + [np.arange(2 * GROUP, 4 * GROUP)])
    block = [np.arange(j * P, (j + 1) * P) for j in range(D_FF // P * 2)]

    arrays = {}
    arrays["x"] = v["x"][0].T.reshape(KT, P, SEQ).transpose(1, 0, 2)
    arrays["mem"] = v["mem"][0].T.reshape(KT, P, N_MEM).transpose(1, 0, 2)
    arrays["pos"] = np.broadcast_to(v["positions"].astype(np.int32), (P, SEQ))
    const = constants()
    const[:, K_G0:K_G0 + KT] = feature_major(v["norm_mix_g"][0])
    const[:, K_GF:K_GF + KT] = feature_major(v["final_norm_g"])
    arrays["const"] = const

    par = np.zeros((L, P, NPAR), np.float32)
    par[:, :, C_XG:C_XG + KT] = feature_major(v["norm_xattn_g"])
    par[:, :, C_MG:C_MG + KT] = feature_major(v["norm_mem_g"])
    par[:, :, C_FG:C_FG + KT] = feature_major(v["norm_ffn_g"])
    for l in range(L):
        par[l, :, C_AG:C_AG + KT] = feature_major(v["norm_mix_g"][l + 1] if l + 1 < L else v["final_norm_g"])
    par[:, :, C_GG:C_GG + KT] = feature_major(v["group_norm_g"][:, order])
    par[:, :, C_DW:C_DB] = v["conv_dw_w"].reshape(L, CONV_WIDTH, GT, P).transpose(0, 3, 2, 1).reshape(L, P, -1)
    for c, name in ((C_DB, "conv_dw_b"), (C_LG, "conv_ln_g"), (C_LB, "conv_ln_b"), (C_PB, "conv_pw_b")):
        par[:, :, c:c + GT] = feature_major(v[name])
    for j in range(4):
        for c in range(4):
            par[:, :, C_SK + 4 * j + c] = v["swa_sinks"][:, j + 4 * (c % 2)][:, None]
    arrays["par"] = par

    q, k = np.arange(P)[:, None], np.arange(2 * P)[None, :] - P
    later = k // HD > q // HD
    index = np.clip(q - k, -MAX_REL, MAX_REL) + MAX_REL
    rel = v["ca_rel_bias"][:, :, index]
    rel[:, :, later] = NEG
    arrays["bias"] = rel.reshape(L, 4, 2, P, 2 * P).transpose(0, 1, 3, 2, 4)
    window = np.where(later | (k // HD < q // HD - 1), np.float32(NEG), np.float32(0))
    arrays["win_mask"] = np.stack([window, window], 1)

    win = win_columns()
    arrays["w_main"] = np.stack([np.concatenate([tiles_of(v["w_in"][l], win), tiles_of(v["w_xkv"][l], block[:8])])
                                 for l in range(L)])
    arrays["w_pw"] = np.stack([tiles_of(v["conv_pw_w"][l], block[:4]) for l in range(L)])
    arrays["w_out"] = np.stack([tiles_of(v["w_out"][l][order], block[:16]) for l in range(L)])
    arrays["w_xq"] = np.stack([tiles_of(v["w_xq"][l], block[:4]) for l in range(L)])
    arrays["w_xo"] = np.stack([tiles_of(v["w_xo"][l], block[:16]) for l in range(L)])
    nf = D_FF // P
    gu = [c for j in range(nf) for c in (block[j], block[nf + j])]
    arrays["w_gu"] = np.stack([tiles_of(v["w_gate_up"][l], gu) for l in range(L)])\
        .reshape(L, FF_CHUNKS, 2 * FT, P, KT * P)
    arrays["w_dn"] = np.stack([[tiles_of(v["w_down"][l][c * FT * P:(c + 1) * FT * P], block[:16])
                                for c in range(FF_CHUNKS)] for l in range(L)])

    nc = bacc.Bacc("TRN2", target_bir_lowering=False, num_devices=1)
    args = {}
    for name in list(arrays):
        arr = np.ascontiguousarray(arrays.pop(name))
        arrays[f"in_{name}"] = arr
        args[name] = nc.dram_tensor(f"in_{name}", arr.shape, mybir.dt.from_np(arr.dtype), kind="ExternalInput").ap()
    args["out"] = nc.dram_tensor("out", (P, KT, SEQ), F32, kind="ExternalOutput").ap()
    build(nc, args)
    r = run_bass_kernel_spmd(nc, [arrays], core_ids=[0])
    out = np.asarray(r.results[0]["out"])
    return np.ascontiguousarray(out.transpose(2, 1, 0).reshape(1, SEQ, D_MODEL))
```

```python
from contextlib import ExitStack

import numpy as np

import concourse.bass as bass
from concourse import mybir

F32, F32R, I32 = mybir.dt.float32, mybir.dt.float32r, mybir.dt.int32
ALU = mybir.AluOpType
ACT = mybir.ActivationFunctionType
AX_X = mybir.AxisListType.X

P = 128
D_MODEL, SEQ, DEPTH, N_MEM = 2048, 256, 2, 256
KT = D_MODEL // P
GROUP = 512
GT = GROUP // P
HD = 64
SB_HD = 128
CONV_WIDTH = 31
PADW = CONV_WIDTH - 1
D_FF = 5632
FF_CHUNKS = 2
FT = D_FF // P // FF_CHUNKS
MAX_REL = 128
N_REL = 2 * MAX_REL + 1
NEG = -1e30
EPS = 1e-6
LN2PI = 2 * np.pi

T_MK, T_PW, T_MV, T_OUT, T_XQ, T_XO, T_FF = 38, 42, 46, 50, 66, 70, 86
FF_TILES = 2 * FT + KT
TILES = T_FF + FF_CHUNKS * FF_TILES
PIECE = 8
RING = 4
Q_PW, Q_MV, Q_OUT, Q_XQ, Q_XO, Q_FF = 84, 88, 96, 128, 136, 152
DN_PIECES = (8, 8, FT - 16)
FF_PIECES = 4 * FT + 3 * KT
PIECES = Q_FF + FF_CHUNKS * FF_PIECES
assert PIECES % RING == 0 and FF_PIECES % RING == 0 and TILES % 2 == 0

C_XG, C_MG, C_FG, C_AG, C_GG, C_DW = 0, 16, 32, 48, 64, 80
C_DB = C_DW + GT * CONV_WIDTH
C_LG, C_LB, C_PB, C_SK = C_DB + 4, C_DB + 8, C_DB + 12, C_DB + 16
NPAR = C_SK + 16
K_ID, K_TRI, K_ONE, K_ROT, K_MSK, K_INV = 0, 128, 256, 384, 512, 640
K_G0, K_GF = 641, 641 + KT
NCONST = K_GF + KT

U_QA, U_KA, U_VA, U_QC, U_KC, U_VC, U_QB, U_KB, U_VB = 0, 4, 8, 12, 16, 20, 24, 28, 29
U_TILES = 30
U_MEM = 12

NX = 4
N_U = 46
N_S = 16
N_P = 12
N_STAT = 10
ST_X1, ST_MEM, ST_MU, ST_VAR, ST_A, ST_B, ST_D, ST_C, ST_X2, ST_X3 = range(N_STAT)
N_X = 3 * KT

H_A, H_B, H_C = 20, 30, 38
H_VB, H_VC = 31, 39
ROPE_STEPS = [(26, 0), (27, 1), (28, 2), (29, 3), (29, 4)]
ROPE_BANK = (1, 1, 0, 1, 0)
ROPE_FREE = {1: 1, 3: 2, 4: 3}
ROPE_FREE_LW = {0: 2, 2: 3, 3: 4}
H_STAT = {0: ST_X1, 12: ST_MEM, 34: ST_MU, 36: ST_VAR, 39: ST_A, 42: ST_B, 47: ST_D, 48: ST_C}
H_Z = 37
PAIRS = [("B", j) for j in range(4)] + [("C", j) for j in range(4)]
G_C = 3
SPLITS = {39: (ST_A, 0), 42: (ST_B, 1), 47: (ST_D, 2), 48: (ST_C, G_C)}
H_CONV = 9
TAPS = 4


def win_dest(i):
    if i < 8:
        return ("gate", "value")[i % 2], i // 2
    if i < 20:
        return "u", i - 8
    if i < 26:
        return "u", U_QB + i - 20
    return "u", U_QC + i - 26


def u_count(i):
    if i < 8:
        return i // 2 + 1
    if i < T_PW:
        return i - 8 + 5
    if i < T_OUT:
        return i - T_MV + 39
    return i - T_XQ + 43


def tile_pieces(i):
    if T_PW <= i < T_MV:
        return [(Q_PW + i - T_PW, 0, 4)]
    if T_XO <= i < T_FF:
        return [(Q_XO + i - T_XO, 0, 4)]
    if i == T_FF:
        q = Q_FF
    elif i >= T_XQ:
        q = Q_XQ + 2 * (i - T_XQ)
    elif i >= T_OUT:
        q = Q_OUT + 2 * (i - T_OUT)
    elif i >= T_MV:
        q = Q_MV + 2 * (i - T_MV)
    else:
        q = 2 * i
    return [(q, 0, 8), (q + 1, 8, 8)]


def pair_at(t, lag):
    for at, first in ((H_B, 0), (H_C, 4)):
        d = t - lag - at
        if 0 <= d < 8 and d % 2 == 0:
            return first + d // 2
    return None


def head_at(t, lag):
    d = t - lag - H_A
    return d // 2 if 0 <= d < 8 and d % 2 == 0 else None


SCALE_A, SCALE_B = float(SB_HD) ** -0.5, float(HD) ** -0.5
ROUND = 12582912.0
TWO_PI_1 = 6.28125
TWO_PI_2 = float(np.float32(round((2 * np.pi - TWO_PI_1) * 2 ** 20) / 2 ** 20))
TWO_PI_3 = float(np.float32(2 * np.pi - TWO_PI_1 - TWO_PI_2))
PI_IN = 3.1415925
LN_EXP = "natural_log_exp_and_others"
POOL_LINKS, POOL_START = 338, 1
ACT_LINKS, DVE_LINKS, DVE_START = 27, 179, 12


def build(nc, a):
    ctx = ExitStack()
    with ctx:
        def sb(name, shape, dt=F32):
            return ctx.enter_context(nc.sbuf_tensor(name, shape, dt))

        def sem(name):
            return ctx.enter_context(nc.semaphore(name))

        x = sb("x", [P, KT, SEQ])
        act_a = sb("act_a", [P, KT, 2 * SEQ], F32R)
        act_h = sb("act_h", [P, FT, 2 * SEQ], F32R)
        u = sb("u", [P, U_TILES, SEQ])
        raw = sb("raw", [P, RING, PIECE * P])
        w_hi = sb("w_hi", [P, RING, PIECE * P], F32R)
        w_lo = sb("w_lo", [P, RING, PIECE * P], F32R)
        hpad = sb("hpad", [P, GT, PADW + SEQ])
        conv = sb("conv", [P, GT, SEQ])
        prob = sb("prob", [P, 2, 2, 384])
        probt = sb("probt", [P, 2, 384])
        bias = sb("bias", [P, 2, 2, 2 * P])
        cos = sb("cos", [P, SEQ])
        sin = sb("sin", [P, SEQ])
        small = sb("small", [P, 2, SEQ])
        ev = sb("ev", [P, 2, SEQ])
        rx = sb("rx", [P, SEQ])
        rmem = sb("rmem", [P, SEQ])
        rg = sb("rg", [P, SEQ])
        acc = sb("acc", [P, SEQ])
        sq = sb("sq", [P, SEQ])
        par = sb("par", [P, NPAR])
        const = sb("const", [P, NCONST])
        eps = sb("eps", [P, 1])
        nmax = sb("nmax", [P, 2, 4])
        total = sb("total", [P, 2, 4])
        esink = sb("esink", [P, 2, 4])
        tick = sb("tick", [P, 1])
        tick_a = sb("tick_a", [P, 1])

        ps = ctx.enter_context(nc.psum_tensor("ps", [P, 8, 512], F32))
        gemm = [ps[:, 0, :], ps[:, 1, :]]
        stat = ps[:, 2, 0:SEQ]
        score = [ps[:, 3, :], ps[:, 4, :]]
        turn = [ps[:, 5, :], ps[:, 6, :]]
        pv = ps[:, 7, 0:SEQ]
        pv_x = [pv, stat]

        ident = const[:, K_ID:K_ID + P]
        tri = const[:, K_TRI:K_TRI + P]
        ones = const[:, K_ONE:K_ONE + P]
        rot = const[:, K_ROT:K_ROT + P]
        mask = const[:, K_MSK:K_MSK + P]

        def flat(ap):
            return ap.rearrange("p k t -> p (k t)")

        vtok = {"A": flat(u[:, U_VA:U_VA + 4, :]), "C": flat(u[:, U_VC:U_VC + 4, :]),
                "B": u[:, U_VB, :], "X": flat(u[:, U_VA:U_VA + 4, :])}
        prob_x = [flat(prob[:, q, :, :])[:, 0:512] for q in range(2)]
        probt_x = [flat(probt[:, :, :])[:, 0:512], flat(conv[:, 0:2, :])]
        gathered = hpad[:, 0, PADW:]
        squares = [flat(conv[:, :, :])] + [flat(u[:, 4 * h:4 * h + 4, :]) for h in range(3)]
        group_out = {0: [u[:, U_QA + k, :] for k in range(GT)], 1: [u[:, U_QB + k, :] for k in range(GT)],
                     2: [conv[:, k, :] for k in range(GT)], 3: [u[:, U_QC + k, :] for k in range(GT)]}

        def pair_tiles(p):
            g, j = PAIRS[p]
            if g == "B":
                return U_QB + j, U_KB, [vtok["B"][:, t * P:(t + 1) * P] for t in range(2)], 0
            return (U_QC + j, U_KC + j,
                    [vtok["C"][:, t * 512 + j * P:t * 512 + (j + 1) * P] for t in range(2)], (j + 1) % 2)

        def gain(c):
            return par[:, c:c + 1]

        raw_in = [sem(f"raw_in{b}") for b in range(RING)]
        hi_ready = sem("hi_ready")
        lo_ready = sem("lo_ready")
        piece_done = sem("piece_done")
        t_ready = sem("t_ready")
        evac_done = sem("evac_done")
        const_in, par_in, mem_in = sem("const_in"), sem("par_in"), sem("mem_in")
        x_in = [sem(f"x_in{h}") for h in range(4)]
        square_ready = sem("square_ready")
        half_ready = sem("half_ready")
        bias_in = [sem("bias_in0"), sem("bias_in1")]
        out_in = sem("out_in")
        dve_seq, act_seq, pool_seq = sem("dve_seq"), sem("act_seq"), sem("pool_seq")
        par_free_a, par_free_d = sem("par_free_a"), sem("par_free_d")
        u_ready = sem("u_ready")
        last_ready = sem("last_ready")
        conv_ready = sem("conv_ready")
        gate_in, gate_out = sem("gate_in"), sem("gate_out")
        trig_in, trig_out = sem("trig_in"), sem("trig_out")
        x_ready = sem("x_ready")
        xh_ready = sem("xh_ready")
        xg_ready = sem("xg_ready")
        mh_ready, mg_ready = sem("mh_ready"), sem("mg_ready")
        sq_ready = sem("sq_ready")
        st_done = sem("st_done")
        ln_ready = sem("ln_ready")
        r_ready = sem("r_ready")
        z_in = sem("z_in")
        zh_ready, z_ready = sem("zh_ready"), sem("z_ready")
        yd_ready = sem("yd_ready")
        vt_done, vt_ready = sem("vt_done"), sem("vt_ready")
        s_done = sem("s_done")
        sp_ready = sem("sp_ready")
        l1_ready = sem("l1_ready")
        sfx_done = sem("sfx_done")
        lw_ready, we_ready, w_ready = sem("lw_ready"), sem("we_ready"), sem("w_ready")
        rot_done, rope_ready = sem("rot_done"), sem("rope_ready")
        nm_ready = sem("nm_ready")
        e_ready = sem("e_ready")
        p_ready = sem("p_ready")
        tr_done, pt_ready = sem("tr_done"), sem("pt_ready")
        pv_done, y_ready = sem("pv_done"), sem("y_ready")
        yn_ready, yh_ready, yg_ready = sem("yn_ready"), sem("yh_ready"), sem("yg_ready")
        oh_ready, o_ready = sem("oh_ready"), sem("o_ready")
        gs_ready, sil_ready = sem("gs_ready"), sem("sil_ready")
        prod_ready, hh_ready, h_ready = sem("prod_ready"), sem("hh_ready"), sem("h_ready")

        block = ctx.enter_context(nc.Block())

        @block.sync
        def _(sp):
            sp.dma_start(const[:, :], a["const"]).then_inc(const_in, 16)
            sp.dma_start(cos[:, :].bitcast(I32), a["pos"]).then_inc(const_in, 16)

            def piece(start, k, blocks, src):
                sp.wait_ge(lo_ready, start + (k + 1))
                sp.dma_start(raw[:, k % RING, 0:blocks * P], src).then_inc(raw_in[k % RING], 16)

            for h in range(4):
                sp.dma_start(x[:, 4 * h:4 * h + 4, :], a["x"][:, 4 * h:4 * h + 4, :]).then_inc(x_in[h], 16)
                if h % 2 == 0:
                    piece(0, h // 2, PIECE, a["w_main"][0, 0][:, h // 2 * PIECE * P:(h // 2 + 1) * PIECE * P])
            with sp.Fori(0, DEPTH) as l:
                base = l * PIECES

                def pair_bias(buf, src, used):
                    if used:
                        sp.wait_ge(nm_ready, l * N_P + used)
                    sp.dma_start(bias[:, buf, :, :], src).then_inc(bias_in[buf], 16)

                for i in range(T_OUT):
                    if i == H_B - 2:
                        pair_bias(0, a["win_mask"], 0)
                        pair_bias(1, a["bias"][l, 0], 0)
                    for pair in (1, 2, 3):
                        if i == H_C + 2 * pair - (0 if pair != 2 else 1):
                            pair_bias((pair + 1) % 2, a["bias"][l, pair], pair + 3)
                    if i == 0:
                        continue
                    for n, b0, nb in tile_pieces(i):
                        if T_PW <= i < T_MV:
                            src = a["w_pw"][l, i - T_PW]
                        else:
                            src = a["w_main"][l, i if i < T_PW else i - 4][:, b0 * P:(b0 + nb) * P]
                        piece(base, n, nb, src)
                with sp.Fori(0, KT // 2) as j:
                    for k in range(4):
                        piece(base + j * 4 + Q_OUT, k, 8,
                              a["w_out"][l, j * 2 + k // 2][:, (k % 2) * 8 * P:(k % 2 + 1) * 8 * P])
                for k in range(8):
                    piece(base + Q_XQ, k, 8, a["w_xq"][l, k // 2][:, (k % 2) * 8 * P:(k % 2 + 1) * 8 * P])
                with sp.Fori(0, KT // 4) as j:
                    for k in range(4):
                        piece(base + j * 4 + Q_XO, k, 4, a["w_xo"][l, j * 4 + k])
                with sp.Fori(0, FF_CHUNKS) as c:
                    gate = base + c * FF_PIECES + Q_FF
                    down = base + c * FF_PIECES + (Q_FF + 4 * FT)
                    with sp.Fori(0, FT) as j:
                        for k in range(4):
                            piece(gate + j * 4, k, 8,
                                  a["w_gu"][l, c, j * 2 + k // 2][:, (k % 2) * 8 * P:(k % 2 + 1) * 8 * P])
                    with sp.Fori(0, KT // 4) as j:
                        for k in range(12):
                            b0, nb = 8 * (k % 3), DN_PIECES[k % 3]
                            piece(down + j * 12, k, nb, a["w_dn"][l, c, j * 4 + k // 3][:, b0 * P:(b0 + nb) * P])
                for n, b0, nb in tile_pieces(0):
                    piece(base, PIECES + n, nb, a["w_next"][l][:, b0 * P:(b0 + nb) * P])
            for h in range(4):
                if h < 3:
                    sp.wait_ge(x_ready, DEPTH * N_X + 4 * h + 4)
                else:
                    sp.wait_ge(last_ready, 2 * GT)
                sp.dma_start(a["out"][:, 4 * h:4 * h + 4, :], x[:, 4 * h:4 * h + 4, :]).then_inc(out_in, 16)
            sp.wait_ge(out_in, 64)

        @block.gpsimd
        def _(pool):
            seq = [0]

            def link(ins, base):
                seq[0] += 1
                ins.then_inc(pool_seq, 1)
                pool.wait_ge(pool_seq, base + seq[0])

            def square_sum(srcs, base, wait):
                for k, s in enumerate(srcs):
                    wait(k)
                    if k == 0:
                        link(nc.gpsimd.tensor_tensor(acc[:, :], s, s, ALU.mult), base)
                        continue
                    link(nc.gpsimd.tensor_tensor(sq[:, :], s, s, ALU.mult), base)
                    ins = nc.gpsimd.tensor_tensor(acc[:, :], acc[:, :], sq[:, :], ALU.add)
                    if k == len(srcs) - 1:
                        ins.then_inc(sq_ready, 1)
                    else:
                        link(ins, base)

            link(nc.gpsimd.memset(hpad[:, :, 0:PADW], 0.0), 0)
            for h in range(2, 4):
                pool.wait_ge(x_in[h], 16)
                v = flat(x[:, 4 * h:4 * h + 4, :])
                nc.gpsimd.tensor_tensor(squares[h], v, v, ALU.mult).then_inc(half_ready, 1)
            pool.wait_ge(half_ready, 2)
            nc.gpsimd.tensor_tensor(squares[2], squares[2], squares[3], ALU.add).then_inc(half_ready, 1)
            assert seq[0] == POOL_START, seq[0]
            seq[0] = 0
            with pool.Fori(0, DEPTH) as l:
                base = l * POOL_LINKS + POOL_START

                def along(column):
                    return column.broadcast_to([P, SEQ])

                def used_up(n):
                    pool.wait_ge(r_ready, l * N_STAT + n)

                pool.wait_ge(par_free_a, l + 1)
                pool.wait_ge(par_free_d, l + 1)
                pool.dma_start(par[:, :], a["par"][l]).then_inc(par_in, 16)
                pool.dma_start(u[:, U_MEM:U_MEM + KT, :], a["mem"]).then_inc(mem_in, 16)
                pool.wait_ge(mem_in, l * 16 + 16)
                used_up(ST_MEM)
                square_sum([u[:, U_MEM + k, :] for k in range(KT)], base, lambda k: None)
                pool.wait_ge(par_in, l * 16 + 16)
                for j in range(GT - 1):
                    pool.wait_ge(u_ready, l * N_U + u_count(2 * j + 1))
                    for tap in range(CONV_WIDTH):
                        src = hpad[:, j, tap:tap + SEQ]
                        w = gain(C_DW + j * CONV_WIDTH + tap)
                        if tap == 0:
                            link(nc.gpsimd.tensor_tensor(conv[:, j, :], src, along(w), ALU.mult), base)
                            link(nc.gpsimd.tensor_tensor(conv[:, j, :], conv[:, j, :], along(gain(C_DB + j)), ALU.add), base)
                            continue
                        link(nc.gpsimd.tensor_tensor(sq[:, :], src, along(w), ALU.mult), base)
                        link(nc.gpsimd.tensor_tensor(conv[:, j, :], conv[:, j, :], sq[:, :], ALU.add), base)
                used_up(ST_MU)
                pool.wait_ge(conv_ready, l + 1)
                link(nc.gpsimd.tensor_tensor(acc[:, :], conv[:, 0, :], conv[:, 1, :], ALU.add), base)
                link(nc.gpsimd.tensor_tensor(acc[:, :], acc[:, :], conv[:, 2, :], ALU.add), base)
                nc.gpsimd.tensor_tensor(acc[:, :], acc[:, :], conv[:, 3, :], ALU.add).then_inc(sq_ready, 1)
                used_up(ST_VAR)
                square_sum(group_out[2], base, lambda k: None)
                for n, g in ((ST_A, 0), (ST_B, 1)):
                    used_up(n)
                    square_sum(group_out[g], base,
                               lambda k, g=g: pool.wait_ge(y_ready, l * 12 + (4 * g + k + 1)))

                def chunk_square(k):
                    t = group_out[G_C][k]
                    pool.wait_ge(y_ready, l * 12 + (8 + k + 1))
                    if k == 0:
                        link(nc.gpsimd.tensor_tensor(gathered, t, t, ALU.mult), base)
                        return
                    link(nc.gpsimd.tensor_tensor(sq[:, :], t, t, ALU.mult), base)
                    if k < GT - 1:
                        link(nc.gpsimd.tensor_tensor(gathered, gathered, sq[:, :], ALU.add), base)
                    else:
                        used_up(ST_C)
                        nc.gpsimd.tensor_tensor(acc[:, :], gathered, sq[:, :], ALU.add).then_inc(sq_ready, 1)

                chunk_square(0)
                chunk_square(1)
                used_up(ST_D)
                square_sum(group_out[2], base, lambda k: pool.wait_ge(yd_ready, l * GT + (k + 1)))
                pool.wait_ge(sq_ready, l * N_STAT + (ST_D + 1))
                chunk_square(2)
                chunk_square(3)
                for n in range(3):
                    used_up(ST_X2 + n)
                    square_sum([x[:, k, :] for k in range(KT)], base,
                               lambda k, n=n: pool.wait_ge(x_ready, l * N_X + n * KT + k + 1))
            assert seq[0] == POOL_LINKS, seq[0]
            pool.wait_ge(xg_ready, DEPTH * N_X + KT)
            for k in range(3 * GT, KT):
                nc.gpsimd.tensor_scalar(x[:, k, :], x[:, k, :], const[:, K_GF + k:K_GF + k + 1], None, ALU.mult)\
                  .then_inc(last_ready, 1)
            pool.wait_ge(last_ready, GT)
            pool.wait_ge(r_ready, DEPTH * N_STAT + 1)
            for k in range(3 * GT, KT):
                nc.gpsimd.tensor_tensor(x[:, k, :], x[:, k, :], rx[:, :], ALU.mult).then_inc(last_ready, 1)

        @block.scalar
        def _(act):
            seq = [0]

            def link(ins, base):
                seq[0] += 1
                ins.then_inc(act_seq, 1)
                act.wait_ge(act_seq, base + seq[0])

            def high(start, k, blocks):
                b = k % RING
                act.wait_ge(raw_in[b], start * (16 // RING) + (16 * (k // RING) + 16))
                act.wait_ge(piece_done, start + (k + 1))
                nc.scalar.activation(w_hi[:, b, 0:blocks * P], raw[:, b, 0:blocks * P], ACT.Copy)\
                  .then_inc(hi_ready, 1)

            def small_out(i, last, b=None):
                act.wait_ge(piece_done, last + (RING + 1))
                src, dst = gemm[i % 2][:, SEQ:2 * SEQ], small[:, i % 2, :]
                if b is None:
                    nc.scalar.activation(dst, src, ACT.Copy).then_inc(t_ready, 1)
                else:
                    nc.scalar.activation(dst, src, ACT.Identity, bias=b).then_inc(t_ready, 1)

            def guess(l, n, lbase):
                width = D_MODEL if n in (ST_X1, ST_MEM, ST_X2, ST_X3) else GROUP
                dst = {ST_X1: rx, ST_X2: rx, ST_X3: rx, ST_MEM: rmem}.get(n, rg)
                act.wait_ge(st_done, l * N_STAT + (n + 1))
                link(nc.scalar.activation(acc[:, :], stat, ACT.Identity, bias=eps[:, 0:1], scale=1.0 / width), lbase)
                link(nc.scalar.activation(dst[:, :], acc[:, :], ACT.Ln), lbase)
                nc.scalar.activation(dst[:, :], dst[:, :], ACT.Exp, scale=-0.5).then_inc(ln_ready, 1)

            act.preload_act_table_set(LN_EXP)
            act.wait_ge(const_in, 32)
            for k in range(KT):
                if k % 4 == 0:
                    act.wait_ge(x_in[k // 4], 16)
                nc.scalar.activation(act_a[:, k, 0:SEQ], x[:, k, :], ACT.Identity,
                                     scale=const[:, K_G0 + k:K_G0 + k + 1]).then_inc(xh_ready, 1)
                if k in (3, 11):
                    high(0, k // 8, PIECE)
            for h in range(2):
                nc.scalar.activation(squares[h], flat(x[:, 4 * h:4 * h + 4, :]), ACT.Square)\
                  .then_inc(square_ready, 1)
            act.wait_ge(trig_in, 2)
            nc.scalar.activation(cos[:, :], cos[:, :], ACT.Sin).then_inc(trig_out, 1)
            nc.scalar.activation(sin[:, :], sin[:, :], ACT.Sin).then_inc(trig_out, 1)

            with act.Fori(0, DEPTH) as l:
                base = l * PIECES
                lbase = l * ACT_LINKS

                act.preload_act_table_set(LN_EXP)

                def values_out(which, n):
                    act.wait_ge(vt_done, l * 4 + n)
                    v = vtok[which]
                    if which == "B":
                        nc.scalar.activation(v, turn[1][:, 0:2 * P], ACT.Copy).then_inc(vt_ready, 1)
                    else:
                        nc.scalar.activation(v[:, 0:512], turn[0], ACT.Copy)
                        nc.scalar.activation(v[:, 512:1024], turn[1], ACT.Copy).then_inc(vt_ready, 1)

                def exp_pair(p):
                    q = p % 2
                    act.wait_ge(nm_ready, l * N_P + p + 1)
                    if PAIRS[p][0] == "B":
                        nc.scalar.activation(esink[:, q, :], esink[:, q, :], ACT.Exp)
                    for c in range(4):
                        s = prob[:, q, c % 2, 0:256] if c < 2 else prob[:, q, c % 2, 256:384]
                        ins = nc.scalar.activation(s, s, ACT.Exp, bias=nmax[:, q, c:c + 1],
                                                   accum_out=total[:, q, c:c + 1])
                    ins.then_inc(e_ready, 1)

                def attention_out(dst, n):
                    act.wait_ge(pv_done, l * N_S + n + 1)
                    nc.scalar.activation(dst, pv, ACT.Copy).then_inc(y_ready, 1)

                def split_group(g):
                    for k in range(GT):
                        act.wait_ge(yn_ready, l * KT + GT * g + k + 1)
                        nc.scalar.activation(act_a[:, GT * g + k, 0:SEQ], group_out[g][k], ACT.Copy).then_inc(yh_ready, 1)

                for i in range(T_OUT):
                    pieces = tile_pieces(i + 1)
                    high(base, pieces[0][0], pieces[0][2])
                    h = head_at(i, 5)
                    if h is not None:
                        attention_out(u[:, U_QA + h, :], h)
                    p = pair_at(i, 4)
                    if p is not None:
                        attention_out(u[:, pair_tiles(p)[0], :], 4 + p)
                    p = pair_at(i, 3)
                    if p is not None:
                        act.wait_ge(tr_done, l * N_P + p + 1)
                        nc.scalar.activation(probt[:, 0, :], turn[0][:, 0:384], ACT.Copy)
                        nc.scalar.activation(probt[:, 1, :], turn[1][:, 0:384], ACT.Copy).then_inc(pt_ready, 1)
                    if i == H_A + 1:
                        values_out("A", 1)
                    if i == H_VB + 1:
                        values_out("B", 2)
                    if i == H_VC + 1:
                        values_out("C", 3)
                    h = head_at(i, 1)
                    if h is not None:
                        z = prob[:, h % 2, 0, :]
                        act.wait_ge(s_done, l * N_S + h + 1)
                        link(nc.scalar.activation(z, score[h % 2][:, 0:384], ACT.Abs, scale=SCALE_A), lbase)
                        link(nc.scalar.activation(z, z, ACT.Exp, scale=-1.0), lbase)
                        nc.scalar.activation(z, z, ACT.Ln, bias=1.0).then_inc(sp_ready, 1)
                    if i - 2 in SPLITS:
                        split_group(SPLITS[i - 2][1])
                    if i < 8 and i % 2:
                        act.wait_ge(gate_in, l * GT + i // 2 + 1)
                        nc.scalar.activation(conv[:, i // 2, :], conv[:, i // 2, :], ACT.Sigmoid).then_inc(gate_out, 1)

                    for n, _, nb in pieces[1:]:
                        high(base, n, nb)
                    if i == T_OUT - 1:
                        split_group(G_C)
                    small_out(i, base + tile_pieces(i)[-1][0], gain(C_PB + i - T_PW) if T_PW <= i < T_MV else None)

                    if i in H_STAT and H_STAT[i] != ST_MU:
                        guess(l, H_STAT[i], lbase)
                    if i == 2:
                        act.wait_ge(par_in, l * 16 + 16)
                        act.wait_ge(mem_in, l * 16 + 16)
                    if 2 <= i < 2 + KT:
                        k = i - 2
                        nc.scalar.activation(act_h[:, k, 0:SEQ], u[:, U_MEM + k, :], ACT.Identity,
                                             scale=gain(C_MG + k)).then_inc(mh_ready, 1)
                    h = head_at(i, 3)
                    if h is not None:
                        act.wait_ge(lw_ready, l * 4 + h + 1)
                        nc.scalar.activation(prob[:, h % 2, 0, :], prob[:, h % 2, 0, :], ACT.Exp).then_inc(we_ready, 1)
                    p = pair_at(i, 1)
                    if p is not None:
                        exp_pair(p)
                    if i == H_Z:
                        act.wait_ge(z_in, l + 1)
                        for k in range(GT):
                            ins = nc.scalar.activation(conv[:, k, :], conv[:, k, :], ACT.Silu,
                                                       bias=gain(C_LB + k), scale=gain(C_LG + k))
                        link(ins, lbase)
                    if i == H_Z + 1:
                        for k in range(GT):
                            nc.scalar.activation(act_h[:, KT + k, 0:SEQ], conv[:, k, :], ACT.Copy).then_inc(zh_ready, 1)
                    if i in (8, H_Z + 1):
                        act.preload_act_table_set(LN_EXP)
                def residual_high(j, n, dst, g):
                    act.wait_ge(x_ready, l * N_X + n * KT + j + 1)
                    nc.scalar.activation(dst[:, j, 0:SEQ], x[:, j, :], ACT.Identity,
                                         scale=gain(g + j)).then_inc(xh_ready, 1)

                def x_exp(h):
                    q = h % 2
                    act.wait_ge(nm_ready, l * N_P + 8 + h + 1)
                    for t in range(2):
                        v = slice(t * 256, t * 256 + 256)
                        ins = nc.scalar.activation(prob_x[q][:, v], score[q][:, v], ACT.Exp, bias=nmax[:, q, t:t + 1],
                                                   scale=SCALE_A, accum_out=total[:, q, t:t + 1])
                    ins.then_inc(e_ready, 1)

                def x_turned(h):
                    act.wait_ge(tr_done, l * N_P + 8 + h + 1)
                    nc.scalar.activation(probt_x[h % 2], turn[h % 2], ACT.Copy).then_inc(pt_ready, 1)

                def x_high(h):
                    act.wait_ge(pv_done, l * N_S + 12 + h + 1)
                    nc.scalar.activation(act_h[:, h, 0:SEQ], pv_x[h % 2], ACT.Copy).then_inc(oh_ready, 1)

                for i in range(T_OUT, T_XO):
                    for n, _, nb in tile_pieces(i + 1):
                        high(base, n, nb)
                    j = i - T_OUT
                    if 0 < j < KT:
                        residual_high(j - 1, 0, act_h, C_XG)
                    if i == T_XQ + 1:
                        values_out("X", 4)
                    small_out(i, base + tile_pieces(i)[-1][0])
                    if j == KT - 1:
                        residual_high(j, 0, act_h, C_XG)
                    if i == T_XQ:
                        guess(l, ST_X2, lbase)
                    if i == T_XQ + 2:
                        x_exp(0)
                x_turned(0)
                x_exp(1)
                high(base, Q_XO + 1, 4)
                x_exp(2)
                x_turned(1)
                x_exp(3)
                x_high(0)
                x_turned(2)
                x_high(1)
                x_turned(3)
                x_high(2)
                x_high(3)

                for i in range(T_XO, T_FF):
                    j = i - T_XO
                    high(base, Q_XO + j + 2, 4 if j + 2 < KT else PIECE)
                    if j:
                        residual_high(j - 1, 1, act_a, C_FG)
                    small_out(i, base + tile_pieces(i)[-1][0])
                residual_high(KT - 1, 1, act_a, C_FG)

                for c in range(FF_CHUNKS):
                    gate, down = base + (Q_FF + c * FF_PIECES), base + (Q_FF + c * FF_PIECES + 4 * FT)

                    def quad(j, first=False, end=False):
                        at = gate + j * 4
                        for s in range(4):
                            for k in (2 * s + 2, 2 * s + 3):
                                high(at, k, 8)
                            n, q = l * (FF_CHUNKS * FT) + j + (c * FT + s // 2 + 1), s // 2
                            if s % 2:
                                act.wait_ge(gs_ready, n)
                                nc.scalar.activation(conv[:, q, :], conv[:, q, :], ACT.Silu).then_inc(sil_ready, 1)
                            small_out(s, at + (2 * s + 1))
                            if first and s == 0:
                                guess(l, ST_X3, lbase)
                            if s % 2:
                                act.wait_ge(prod_ready, n)
                                nc.scalar.activation(act_h[:, j + q, 0:SEQ], conv[:, 2 + q, :], ACT.Copy).then_inc(hh_ready, 1)

                    quad(0, first=c == 0)
                    with act.Fori(1, FT // 2) as jq:
                        quad(jq * 2)
                    for j in range(KT):
                        high(down, 3 * j + 2, DN_PIECES[2])
                        for k in range(2):
                            high(down, 3 * j + 3 + k, 8)
                        small_out(j, down + (3 * j + 2))
                        if c == FF_CHUNKS - 1:
                            residual_high(j, 2, act_a, C_AG)
                nc.scalar.activation(tick_a[:, :], eps[:, :], ACT.Copy).then_inc(par_free_a, 1)
            assert seq[0] == ACT_LINKS, seq[0]
            act.preload_act_table_set(LN_EXP)
            guess(DEPTH, ST_X1, DEPTH * ACT_LINKS - ACT_LINKS)

        @block.vector
        def _(dve):
            V = nc.vector
            seq = [0]

            def link(ins, base):
                seq[0] += 1
                ins.then_inc(dve_seq, 1)
                dve.wait_ge(dve_seq, base + seq[0])

            def low(start, k, blocks):
                b = k % RING
                dve.wait_ge(hi_ready, start + (k + 1))
                V.tensor_tensor(w_lo[:, b, 0:blocks * P], raw[:, b, 0:blocks * P],
                                w_hi[:, b, 0:blocks * P].bitcast(F32), ALU.subtract).then_inc(lo_ready, 1)

            def add_products(i, number):
                dve.wait_ge(t_ready, number + 1)
                V.tensor_tensor(ev[:, i % 2, :], gemm[i % 2][:, 0:SEQ], small[:, i % 2, :], ALU.add)\
                 .then_inc(evac_done, 1)
                dve.wait_ge(evac_done, number + 3)
                return ev[:, i % 2, :]

            def refine(l, n, lbase, i, final=True):
                dst = {ST_X1: rx, ST_X2: rx, ST_X3: rx, ST_MEM: rmem}.get(n, rg)[:, :]
                tmp = ev[:, (i + 1) % 2, :]
                dve.wait_ge(ln_ready, l * (N_STAT - 1) + (n + 1 if n < ST_MU else n))
                link(V.tensor_tensor(tmp, dst, dst, ALU.mult), lbase)
                link(V.scalar_tensor_tensor(out=tmp, in0=tmp, scalar=-0.5, in1=acc[:, :], op0=ALU.mult, op1=ALU.mult), lbase)
                ins = V.scalar_tensor_tensor(out=dst, in0=tmp, scalar=1.5, in1=dst, op0=ALU.add, op1=ALU.mult)
                if final:
                    ins.then_inc(r_ready, 1)
                    dve.wait_ge(r_ready, l * N_STAT + (n + 1))
                else:
                    link(ins, lbase)

            V.memset(ev[:, 0, :], 0.0).then_inc(lo_ready, RING)
            V.memset(ev[:, 1, :], 0.0).then_inc(piece_done, RING)
            V.memset(esink[:, :, :], 0.0).then_inc(evac_done, 2)
            V.memset(nmax[:, :, :], 0.0).then_inc(par_free_a, 1)
            V.memset(total[:, :, :], 0.0).then_inc(par_free_d, 1)
            link(V.memset(eps[:, :], EPS), 0)
            dve.wait_ge(const_in, 32)
            link(V.tensor_copy(sin[:, :], cos[:, :].bitcast(I32)), 0)
            link(V.tensor_scalar(sin[:, :], sin[:, :], const[:, K_INV:K_INV + 1], None, ALU.mult), 0)
            n = ev[:, 0, :]
            link(V.tensor_scalar(n, sin[:, :], 1.0 / (2 * np.pi), ROUND, ALU.mult, ALU.add), 0)
            link(V.tensor_scalar(n, n, ROUND, None, ALU.subtract), 0)
            for part in (TWO_PI_1, TWO_PI_2, TWO_PI_3):
                link(V.scalar_tensor_tensor(out=sin[:, :], in0=n, scalar=-part, in1=sin[:, :], op0=ALU.mult, op1=ALU.add), 0)
            V.tensor_scalar(sin[:, :], sin[:, :], PI_IN, -PI_IN, ALU.min, ALU.max).then_inc(trig_in, 1)
            dve.wait_ge(trig_in, 1)
            link(V.scalar_tensor_tensor(out=cos[:, :], in0=sin[:, :], scalar=-1.0, in1=sin[:, :], op0=ALU.mult, op1=ALU.min), 0)
            V.tensor_scalar(cos[:, :], cos[:, :], np.pi / 2, None, ALU.add).then_inc(trig_in, 1)
            for k in range(KT):
                if k in (0, 8):
                    low(0, k // 8, PIECE)
                dve.wait_ge(xh_ready, k + 1)
                V.scalar_tensor_tensor(out=act_a[:, k, SEQ:2 * SEQ], in0=x[:, k, :],
                                       scalar=const[:, K_G0 + k:K_G0 + k + 1], in1=act_a[:, k, 0:SEQ].bitcast(F32),
                                       op0=ALU.mult, op1=ALU.subtract).then_inc(xg_ready, 1)
            s4 = squares[0]
            dve.wait_ge(square_ready, 2)
            for h in (1, 2):
                if h == 2:
                    dve.wait_ge(half_ready, 3)
                link(V.tensor_tensor(s4, s4, squares[h], ALU.add), 0)
            link(V.tensor_tensor(s4[:, 0:512], s4[:, 0:512], s4[:, 512:1024], ALU.add), 0)
            V.tensor_tensor(acc[:, :], s4[:, 0:SEQ], s4[:, SEQ:2 * SEQ], ALU.add).then_inc(sq_ready, 1)
            assert seq[0] == DVE_START, seq[0]
            seq[0] = 0

            with dve.Fori(0, DEPTH) as l:
                base = l * PIECES
                tile0 = l * TILES
                lbase = l * DVE_LINKS + DVE_START

                def rope(i, k):
                    t, tmp = u[:, U_QB + k, :], ev[:, i % 2, :]
                    dve.wait_ge(trig_out, 2)
                    dve.wait_ge(rot_done, l * 5 + k + 1)
                    link(V.tensor_tensor(tmp, turn[ROPE_BANK[k]][:, 0:SEQ], sin[:, :], ALU.mult), lbase)
                    link(V.tensor_tensor(t, t, cos[:, :], ALU.mult), lbase)
                    V.tensor_tensor(t, t, tmp, ALU.add).then_inc(rope_ready, 1)
                    dve.wait_ge(rope_ready, l * 5 + k + 1)

                def diagonal(ap):
                    v = ap.rearrange("p (b q) -> p b q", q=P)[:, 0:3:2, :]
                    return v, mask[:, None, :].broadcast_to([P, 2, P])

                def log_beta(h):
                    z, sp_, ls, l1 = score[h % 2][:, 0:384], prob[:, h % 2, 0, :], prob[:, h % 2, 1, :], probt[:, h % 2, :]
                    dve.wait_ge(sp_ready, l * 4 + h + 1)
                    link(V.tensor_scalar(ls, z, SCALE_A, 0.0, ALU.mult, ALU.min), lbase)
                    link(V.tensor_tensor(ls, ls, sp_, ALU.subtract), lbase)
                    link(V.scalar_tensor_tensor(out=l1, in0=z, scalar=-SCALE_A, in1=ls, op0=ALU.mult, op1=ALU.add), lbase)
                    d, m = diagonal(l1)
                    V.tensor_tensor(d, d, m, ALU.mult).then_inc(l1_ready, 1)

                def mask_weights(h):
                    d, m = diagonal(prob[:, h % 2, 0, :])
                    dve.wait_ge(we_ready, l * 4 + h + 1)
                    V.tensor_tensor(d, d, m, ALU.mult).then_inc(w_ready, 1)

                def probabilities(p):
                    q = p % 2
                    dve.wait_ge(e_ready, l * N_P + p + 1)
                    if PAIRS[p][0] == "B":
                        link(V.tensor_tensor(total[:, q, :], total[:, q, :], esink[:, q, :], ALU.add), lbase)
                    link(V.reciprocal(total[:, q, :], total[:, q, :]), lbase)
                    for c in range(4):
                        s = prob[:, q, c % 2, 0:256] if c < 2 else prob[:, q, c % 2, 256:384]
                        ins = V.tensor_scalar(s, s, total[:, q, c:c + 1], None, ALU.mult)
                    ins.then_inc(p_ready, 1)

                def masked_scores(p):
                    q = p % 2
                    b = pair_tiles(p)[3]
                    uses = {0: 3, 1: 2}[b]
                    nth = {0: 1, 1: 1, 2: 1, 3: 1, 4: 1, 5: 2, 6: 2, 7: 3}[p]
                    dve.wait_ge(bias_in[b], l * (16 * uses) + 16 * nth)
                    dve.wait_ge(s_done, l * N_S + 4 + p + 1)
                    for hh in range(2):
                        for lo_, hi_, src in ((0, 256, bias[:, b, hh, :]), (256, 384, bias[:, b, hh, P:2 * P])):
                            ins = V.scalar_tensor_tensor(out=prob[:, q, hh, lo_:hi_], in0=score[hh][:, lo_:hi_],
                                                         scalar=SCALE_B, in1=src, op0=ALU.mult, op1=ALU.add)
                    link(ins, lbase)
                    ins = V.tensor_reduce(nmax[:, q, 0:2], prob[:, q, :, 0:256], AX_X, ALU.max, negate=True)
                    ins = V.tensor_reduce(nmax[:, q, 2:4], prob[:, q, :, 256:384], AX_X, ALU.max, negate=True)
                    if PAIRS[p][0] == "B":
                        sink = par[:, C_SK + 4 * p:C_SK + 4 * p + 4]
                        link(ins, lbase)
                        link(V.tensor_scalar(esink[:, q, :], sink, -1.0, None, ALU.mult), lbase)
                        link(V.tensor_tensor(nmax[:, q, :], nmax[:, q, :], esink[:, q, :], ALU.min), lbase)
                        ins = V.tensor_tensor(esink[:, q, :], sink, nmax[:, q, :], ALU.add)
                    ins.then_inc(nm_ready, 1)

                def conv_taps(i):
                    first = TAPS * (i - H_CONV)
                    if not 0 <= first < CONV_WIDTH:
                        return
                    row = conv[:, GT - 1, :]
                    for tap in range(first, min(first + TAPS, CONV_WIDTH)):
                        src, w = hpad[:, GT - 1, tap:tap + SEQ], gain(C_DW + (GT - 1) * CONV_WIDTH + tap)
                        if tap == 0:
                            ins = V.tensor_scalar(row, src, w, gain(C_DB + GT - 1), ALU.mult, ALU.add)
                        else:
                            ins = V.scalar_tensor_tensor(out=row, in0=src, scalar=w, in1=row, op0=ALU.mult, op1=ALU.add)
                        if tap < CONV_WIDTH - 1:
                            link(ins, lbase)
                        else:
                            ins.then_inc(conv_ready, 1)

                def normalise(g):
                    for k in range(GT):
                        t = group_out[g][k]
                        ins = V.scalar_tensor_tensor(out=t, in0=t, scalar=gain(C_GG + GT * g + k), in1=rg[:, :],
                                                     op0=ALU.mult, op1=ALU.mult)
                        ins.then_inc(yn_ready, 1)
                    dve.wait_ge(yn_ready, l * KT + GT * g + GT)
                    V.memset(tick[:, :], 0.0).then_inc(r_ready, 1)

                def split_group(g):
                    for k in range(GT):
                        dve.wait_ge(yh_ready, l * KT + GT * g + k + 1)
                        V.tensor_tensor(act_a[:, GT * g + k, SEQ:2 * SEQ], group_out[g][k],
                                        act_a[:, GT * g + k, 0:SEQ].bitcast(F32), ALU.subtract).then_inc(yg_ready, 1)

                for i in range(T_OUT):
                    h = head_at(i, 4)
                    if h is not None:
                        mask_weights(h)
                    h = head_at(i, 3)
                    if h is not None:
                        dve.wait_ge(sfx_done, l * 4 + h + 1)
                        V.tensor_tensor(prob[:, h % 2, 0, :], turn[h % 2][:, 0:384], prob[:, h % 2, 1, :], ALU.add)\
                         .then_inc(lw_ready, 1)
                    p = pair_at(i, 2)
                    if p is not None:
                        probabilities(p)
                    p = pair_at(i, 1)
                    if p is not None:
                        masked_scores(p)
                    pieces = tile_pieces(i + 1)
                    low(base, pieces[0][0], pieces[0][2])
                    if i == 3:
                        dve.wait_ge(par_in, l * 16 + 16)
                        dve.wait_ge(mem_in, l * 16 + 16)
                    if 3 <= i < 3 + KT:
                        k = i - 3
                        dve.wait_ge(mh_ready, l * KT + k + 1)
                        V.scalar_tensor_tensor(out=act_h[:, k, SEQ:2 * SEQ], in0=u[:, U_MEM + k, :], scalar=gain(C_MG + k),
                                               in1=act_h[:, k, 0:SEQ].bitcast(F32), op0=ALU.mult,
                                               op1=ALU.subtract).then_inc(mg_ready, 1)
                    h = head_at(i, 1)
                    if h is not None:
                        log_beta(h)
                    for t, k in ROPE_STEPS:
                        if i == t + 1:
                            rope(i, k)
                    if i - 1 in SPLITS:
                        refine(l, SPLITS[i - 1][0], lbase, i - 1, final=False)
                        normalise(SPLITS[i - 1][1])
                    if i - 2 in SPLITS:
                        split_group(SPLITS[i - 2][1])
                    if H_STAT.get(i - 1) == ST_MEM:
                        refine(l, ST_MEM, lbase, i - 1)
                    if H_STAT.get(i - 1) == ST_MU:
                        dve.wait_ge(st_done, l * N_STAT + ST_MU + 1)
                        for k in range(GT):
                            ins = V.scalar_tensor_tensor(out=conv[:, k, :], in0=stat, scalar=-1.0 / GROUP,
                                                         in1=conv[:, k, :], op0=ALU.mult, op1=ALU.add)
                        ins.then_inc(r_ready, 1)
                    if H_STAT.get(i - 1) == ST_VAR:
                        refine(l, ST_VAR, lbase, i - 1, final=False)
                        for k in range(GT):
                            ins = V.tensor_tensor(conv[:, k, :], conv[:, k, :], rg[:, :], ALU.mult)
                        ins.then_inc(z_in, 1)
                        dve.wait_ge(z_in, l + 1)
                        V.memset(tick[:, :], 0.0).then_inc(r_ready, 1)
                    if i == H_Z + 3:
                        for k in range(GT):
                            dve.wait_ge(zh_ready, l * GT + k + 1)
                            V.tensor_tensor(act_h[:, KT + k, SEQ:2 * SEQ], conv[:, k, :],
                                            act_h[:, KT + k, 0:SEQ].bitcast(F32), ALU.subtract).then_inc(z_ready, 1)

                    for n, _, nb in pieces[1:]:
                        low(base, n, nb)
                    if i == T_OUT - 1:
                        split_group(G_C)
                    s = add_products(i, tile0 + i)
                    if H_STAT.get(i) == ST_X1:
                        refine(l, ST_X1, lbase, i)
                    if i < T_MK:
                        kind, j = win_dest(i)
                        if kind == "gate":
                            V.tensor_tensor(conv[:, j, :], s, rx[:, :], ALU.mult).then_inc(gate_in, 1)
                        elif kind == "value":
                            link(V.tensor_tensor(s, s, rx[:, :], ALU.mult), lbase)
                            dve.wait_ge(gate_out, l * GT + j + 1)
                            V.tensor_tensor(hpad[:, j, PADW:], s, conv[:, j, :], ALU.mult).then_inc(u_ready, 1)
                        else:
                            V.tensor_tensor(u[:, j, :], s, rx[:, :], ALU.mult).then_inc(u_ready, 1)
                    elif T_PW <= i < T_MV:
                        V.tensor_copy(conv[:, i - T_PW, :], s).then_inc(yd_ready, 1)
                    else:
                        j = U_KA + i - T_MK if i < T_PW else U_VA + i - T_MV
                        V.tensor_tensor(u[:, j, :], s, rmem[:, :], ALU.mult).then_inc(u_ready, 1)
                    conv_taps(i)
                def residual(j, s, number):
                    ins = V.tensor_tensor(x[:, j, :], x[:, j, :], s, ALU.add)
                    if number is None:
                        link(ins, lbase)
                    else:
                        ins.then_inc(x_ready, 1)

                def residual_low(j, n, dst, g):
                    dve.wait_ge(xh_ready, l * N_X + (KT + n * KT + j + 1))
                    V.scalar_tensor_tensor(out=dst[:, j, SEQ:2 * SEQ], in0=x[:, j, :], scalar=gain(g + j),
                                           in1=dst[:, j, 0:SEQ].bitcast(F32), op0=ALU.mult,
                                           op1=ALU.subtract).then_inc(xg_ready, 1)

                def x_max(h):
                    q = h % 2
                    dve.wait_ge(s_done, l * N_S + 12 + h + 1)
                    link(V.tensor_reduce(nmax[:, q, 0:2], score[q].rearrange("p (t k) -> p t k", t=2), AX_X, ALU.max,
                                         negate=True), lbase)
                    V.tensor_scalar(nmax[:, q, 0:2], nmax[:, q, 0:2], SCALE_A, None, ALU.mult).then_inc(nm_ready, 1)

                def x_prob(h):
                    q = h % 2
                    dve.wait_ge(e_ready, l * N_P + 8 + h + 1)
                    link(V.reciprocal(total[:, q, 0:2], total[:, q, 0:2]), lbase)
                    for t in range(2):
                        s = prob_x[q][:, t * 256:t * 256 + 256]
                        ins = V.tensor_scalar(s, s, total[:, q, t:t + 1], None, ALU.mult)
                    ins.then_inc(p_ready, 1)

                def x_low(h):
                    dve.wait_ge(oh_ready, l * NX + h + 1)
                    V.tensor_tensor(act_h[:, h, SEQ:2 * SEQ], pv_x[h % 2], act_h[:, h, 0:SEQ].bitcast(F32), ALU.subtract)\
                     .then_inc(o_ready, 1)

                for i in range(T_OUT, T_XO):
                    for n, _, nb in tile_pieces(i + 1):
                        low(base, n, nb)
                    if i == T_XQ + 2:
                        x_max(0)
                    if i == T_XQ + 3:
                        x_prob(0)
                        x_max(1)
                    if i < T_XQ:
                        j = i - T_OUT
                        if j:
                            residual_low(j - 1, 0, act_h, C_XG)
                        residual(j, add_products(i, tile0 + i), 0)
                        if j == KT - 1:
                            residual_low(j, 0, act_h, C_XG)
                    else:
                        s = add_products(i, tile0 + i)
                        if i == T_XQ:
                            refine(l, ST_X2, lbase, i)
                        V.tensor_tensor(u[:, U_QC + i - T_XQ, :], s, rx[:, :], ALU.mult).then_inc(u_ready, 1)

                x_max(2)
                x_prob(1)
                low(base, Q_XO + 1, 4)
                x_max(3)
                x_prob(2)
                x_low(0)
                x_prob(3)
                x_low(1)
                x_low(2)
                x_low(3)

                for i in range(T_XO, T_FF):
                    j = i - T_XO
                    low(base, Q_XO + j + 2, 4 if j + 2 < KT else PIECE)
                    if j:
                        residual_low(j - 1, 1, act_a, C_FG)
                    residual(j, add_products(i, tile0 + i), 1)
                residual_low(KT - 1, 1, act_a, C_FG)

                for c in range(FF_CHUNKS):
                    gate, down = base + (Q_FF + c * FF_PIECES), base + (Q_FF + c * FF_PIECES + 4 * FT)
                    first_tile = T_FF + c * FF_TILES

                    def quad(j, lb, first=False):
                        at = gate + j * 4
                        for s in range(4):
                            for k in (2 * s + 2, 2 * s + 3):
                                low(at, k, 8)
                            e = add_products(s, tile0 + j * 2 + (first_tile + s))
                            if first and s == 0:
                                refine(l, ST_X3, lb, s)
                            n, q = l * (FF_CHUNKS * FT) + j + (c * FT + s // 2 + 1), s // 2
                            if s % 2 == 0:
                                V.tensor_tensor(conv[:, q, :], e, rx[:, :], ALU.mult).then_inc(gs_ready, 1)
                            else:
                                link(V.tensor_tensor(e, e, rx[:, :], ALU.mult), lb)
                                dve.wait_ge(sil_ready, n)
                                V.tensor_tensor(conv[:, 2 + q, :], conv[:, q, :], e, ALU.mult).then_inc(prod_ready, 1)
                                dve.wait_ge(hh_ready, n)
                                V.tensor_tensor(act_h[:, j + q, SEQ:2 * SEQ], conv[:, 2 + q, :],
                                                act_h[:, j + q, 0:SEQ].bitcast(F32), ALU.subtract).then_inc(h_ready, 1)

                    quad(0, lbase, first=c == 0)
                    before = seq[0]
                    with dve.Fori(1, FT // 2) as jq:
                        quad(jq * 2, lbase + jq * 2 - 2)
                    assert seq[0] == before + 2
                    seq[0] = before + 2 * (FT // 2 - 1)
                    for j in range(KT):
                        low(down, 3 * j + 2, DN_PIECES[2])
                        for k in range(2):
                            low(down, 3 * j + 3 + k, 8)
                        last_chunk = c == FF_CHUNKS - 1
                        if j and last_chunk:
                            residual_low(j - 1, 2, act_a, C_AG)
                        s = add_products(j, tile0 + (first_tile + 2 * FT + j))
                        residual(j, s, 2 if last_chunk else None)
                residual_low(KT - 1, 2, act_a, C_AG)
                dve.wait_ge(xg_ready, l * N_X + 4 * KT)
                V.memset(tick[:, :], 0.0).then_inc(par_free_d, 1)
            assert seq[0] == DVE_LINKS, seq[0]
            seq[0] = 0
            refine(DEPTH, ST_X1, DEPTH * DVE_LINKS + DVE_START, 0)
            for k in range(3 * GT):
                V.scalar_tensor_tensor(out=x[:, k, :], in0=x[:, k, :], scalar=const[:, K_GF + k:K_GF + k + 1],
                                       in1=rx[:, :], op0=ALU.mult, op1=ALU.mult).then_inc(x_ready, 1)

        @block.tensor
        def _(pe):
            T = nc.tensor

            def tile(start, number, pieces, rhs, bank, ready=None):
                pe.wait_ge(evac_done, number + 1)
                last = pieces[-1][1] + pieces[-1][2] - 1
                for n, b0, nb in pieces:
                    pe.wait_ge(lo_ready, start + (n + RING + 1))
                    for k in range(nb):
                        kk = b0 + k
                        if ready is not None:
                            ready(kk)
                        w = slice(k * P, (k + 1) * P)
                        if kk < last:
                            T.matmul(bank, w_hi[:, n % RING, w], rhs[:, kk, :], start=kk == 0, stop=False)
                        ins = T.matmul(bank[:, SEQ:2 * SEQ], w_lo[:, n % RING, w], rhs[:, kk, 0:SEQ],
                                       start=False, stop=False)
                        if kk == last:
                            ins = T.matmul(bank, w_hi[:, n % RING, w], rhs[:, kk, :], start=False, stop=True)
                    ins.then_inc(piece_done, 1)

            def statistic(l, n):
                pe.wait_ge(sq_ready, l * N_STAT + (n + 1))
                T.matmul(stat, ones, acc[:, :], start=True, stop=True).then_inc(st_done, 1)

            pe.wait_ge(const_in, 32)
            with pe.Fori(0, DEPTH) as l:
                base, tile0 = l * PIECES, l * TILES

                def turn_values(which, n, ready):
                    pe.wait_ge(u_ready, l * N_U + ready)
                    if which == "B":
                        pe.wait_ge(rope_ready, l * 5 + 4)
                        for t in range(2):
                            ins = T.transpose(turn[1][:, t * P:(t + 1) * P], u[:, U_VB, t * P:(t + 1) * P], ident)
                    else:
                        first = U_VC if which == "C" else U_VA
                        for t in range(2):
                            for j in range(4):
                                ins = T.transpose(turn[t][:, j * P:(j + 1) * P], u[:, first + j, t * P:(t + 1) * P], ident)
                    ins.then_inc(vt_done, 1)

                def head_scores(h):
                    pe.wait_ge(u_ready, l * N_U + u_count(19))
                    q, k = u[:, U_QA + h, :], u[:, U_KA + h, :]
                    T.matmul(score[h % 2][:, 0:256], k[:, 0:P], q, start=True, stop=True)
                    T.matmul(score[h % 2][:, 256:384], k[:, P:2 * P], q[:, P:2 * P], start=False, stop=True,
                             skip_group_check=True).then_inc(s_done, 1)

                def head_suffix(h):
                    l1 = probt[:, h % 2, :]
                    pe.wait_ge(vt_ready, l * 4 + 1)
                    pe.wait_ge(l1_ready, l * 4 + h + 1)
                    if h == 3:
                        pe.wait_ge(rope_ready, l * 5 + 2)
                    T.matmul(turn[h % 2][:, P:2 * P], ones, l1[:, 256:384], start=True, stop=False)
                    T.matmul(turn[h % 2][:, P:2 * P], tri, l1[:, P:2 * P], start=False, stop=True)
                    for v in (slice(0, P), slice(2 * P, 3 * P)):
                        ins = T.matmul(turn[h % 2][:, v], tri, l1[:, v], start=False, stop=True, skip_group_check=True)
                    ins.then_inc(sfx_done, 1)

                def head_output(h):
                    w = prob[:, h % 2, 0, :]
                    pe.wait_ge(w_ready, l * 4 + h + 1)
                    if h:
                        pe.wait_ge(y_ready, l * 12 + h)
                    T.matmul(pv[:, P:2 * P], vtok["A"][:, 512 + h * P:512 + (h + 1) * P], w[:, 256:384],
                             start=True, stop=False)
                    T.matmul(pv[:, P:2 * P], vtok["A"][:, h * P:(h + 1) * P], w[:, P:2 * P], start=False, stop=True)
                    T.matmul(pv[:, 0:P], vtok["A"][:, h * P:(h + 1) * P], w[:, 0:P], start=False, stop=True,
                             skip_group_check=True).then_inc(pv_done, 1)

                def rotate(k):
                    pe.wait_ge(u_ready, l * N_U + u_count(25))
                    if k in ROPE_FREE:
                        pe.wait_ge(rope_ready, l * 5 + ROPE_FREE[k])
                    if k in ROPE_FREE_LW:
                        pe.wait_ge(lw_ready, l * 4 + ROPE_FREE_LW[k])
                    T.matmul(turn[ROPE_BANK[k]][:, 0:SEQ], rot, u[:, U_QB + k, :], start=True, stop=True).then_inc(rot_done, 1)

                def pair_scores(p):
                    tq, tk, _, _ = pair_tiles(p)
                    if PAIRS[p][0] == "B":
                        pe.wait_ge(rope_ready, l * 5 + 5)
                    else:
                        pe.wait_ge(u_ready, l * N_U + u_count(37))
                    for hh in range(2):
                        v = slice(64 * hh, 64 * hh + 64)
                        T.matmul(score[hh][:, 0:256], u[v, tq, P:2 * P], u[v, tk, :], start=True, stop=True)
                        ins = T.matmul(score[hh][:, 256:384], u[v, tq, 0:P], u[v, tk, 0:P], start=False, stop=True,
                                       skip_group_check=True)
                    ins.then_inc(s_done, 1)

                def pair_turn(p):
                    pe.wait_ge(vt_ready, l * 4 + (2 if p < 4 else 3))
                    pe.wait_ge(p_ready, l * N_P + p + 1)
                    for hh in range(2):
                        s = prob[:, p % 2, hh, :]
                        T.transpose(turn[hh][:, 0:P], s[:, 256:384], ident)
                        T.transpose(turn[hh][:, P:2 * P], s[:, 0:P], ident)
                        ins = T.transpose(turn[hh][:, 2 * P:3 * P], s[:, P:2 * P], ident)
                    ins.then_inc(tr_done, 1)

                def pair_output(p):
                    _, _, v, _ = pair_tiles(p)
                    pe.wait_ge(pt_ready, l * N_P + p + 1)
                    pe.wait_ge(y_ready, l * 12 + 4 + p)
                    for hh in range(2):
                        rows = slice(64 * hh, 64 * hh + 64)
                        T.matmul(pv[rows, P:2 * P], v[1][:, rows], probt[:, hh, 256:384], start=True, stop=False)
                        T.matmul(pv[rows, P:2 * P], v[0][:, rows], probt[:, hh, P:2 * P], start=False, stop=True)
                        ins = T.matmul(pv[rows, 0:P], v[0][:, rows], probt[:, hh, 0:P], start=False, stop=True,
                                       skip_group_check=True)
                    ins.then_inc(pv_done, 1)

                for i in range(T_OUT):
                    ready, rhs = None, act_a
                    if i == 0:
                        ready = lambda k: pe.wait_ge(xg_ready, l * N_X + k + 1)
                    if i == T_MK:
                        pe.wait_ge(mg_ready, l * KT + KT)
                    if i >= T_MK:
                        rhs = act_h
                    if T_PW <= i < T_MV:
                        rhs = act_h[:, KT:KT + GT, :]
                        if i == T_PW:
                            pe.wait_ge(z_ready, l * GT + GT)
                    tile(base, tile0 + i, tile_pieces(i), rhs, gemm[i % 2], ready)
                    if i in H_STAT:
                        statistic(l, H_STAT[i])
                    h = head_at(i, 4)
                    if h is not None:
                        head_output(h)
                    h = head_at(i, 2)
                    if h is not None:
                        head_suffix(h)
                    if i == H_A:
                        turn_values("A", 1, u_count(19))
                    h = head_at(i, 0)
                    if h is not None:
                        head_scores(h)
                    for t, k in ROPE_STEPS:
                        if i == t:
                            rotate(k)
                    p = pair_at(i, 3)
                    if p is not None:
                        pair_output(p)
                    if i == H_VB:
                        turn_values("B", 2, u_count(25))
                    if i == H_VC:
                        turn_values("C", 3, u_count(37))
                    p = pair_at(i, 2)
                    if p is not None:
                        pair_turn(p)
                    p = pair_at(i, 0)
                    if p is not None:
                        pair_scores(p)

                with pe.Fori(0, KT // 2) as j:
                    for s in range(2):
                        ready = (lambda k: pe.wait_ge(yg_ready, l * KT + max(k, GT) + GT) if k in (0, 8, 12) else None) \
                            if s == 0 else None
                        tile(base + j * 4 + Q_OUT, tile0 + j * 2 + (T_OUT + s), [(2 * s, 0, 8), (2 * s + 1, 8, 8)],
                             act_a, gemm[s], ready)
                def x_scores(h):
                    q, k = u[:, U_QC + h, :], u[:, U_KA + h, :]
                    pe.wait_ge(u_ready, l * N_U + u_count(T_XQ + h))
                    for t in range(2):
                        ins = T.matmul(score[h % 2][:, t * 256:t * 256 + 256], q[:, t * P:(t + 1) * P], k,
                                       start=t == 0, stop=True, skip_group_check=True)
                    ins.then_inc(s_done, 1)

                def x_turn(h):
                    pe.wait_ge(p_ready, l * N_P + 8 + h + 1)
                    for k in range(2):
                        for t in range(2):
                            ins = T.transpose(turn[h % 2][:, k * 256 + t * P:k * 256 + (t + 1) * P],
                                              prob_x[h % 2][:, t * 256 + k * P:t * 256 + (k + 1) * P], ident)
                    ins.then_inc(tr_done, 1)

                def x_output(h):
                    pe.wait_ge(pt_ready, l * N_P + 8 + h + 1)
                    if h >= 2:
                        pe.wait_ge(o_ready, l * NX + (h - 1))
                    for t in range(2):
                        ins = T.matmul(pv_x[h % 2], vtok["X"][:, t * 512 + h * P:t * 512 + (h + 1) * P],
                                       probt_x[h % 2][:, t * 256:t * 256 + 256], start=t == 0, stop=t == 1)
                    ins.then_inc(pv_done, 1)

                for i in range(T_XQ, T_XO):
                    ready = (lambda k: pe.wait_ge(xg_ready, l * N_X + KT + k + 1)) if i == T_XQ else None
                    tile(base, tile0 + i, tile_pieces(i), act_h, gemm[i % 2], ready)
                    if i == T_XQ:
                        statistic(l, ST_X2)
                        turn_values("X", 4, u_count(T_OUT - 1))
                    if i == T_XQ + 1:
                        x_scores(0)
                    if i == T_XQ + 2:
                        x_scores(1)
                pe.wait_ge(vt_ready, l * 4 + 4)
                x_turn(0)
                x_scores(2)
                x_turn(1)
                x_scores(3)
                x_output(0)
                x_turn(2)
                x_output(1)
                x_turn(3)
                x_output(2)
                x_output(3)

                for i in range(T_XO, T_FF):
                    ready = (lambda k: pe.wait_ge(o_ready, l * NX + k + 1)) if i == T_XO else None
                    tile(base, tile0 + i, tile_pieces(i), act_h, gemm[i % 2], ready)

                for c in range(FF_CHUNKS):
                    first_tile, piece0 = T_FF + c * FF_TILES, Q_FF + c * FF_PIECES

                    def quad(j, first=False):
                        for s in range(4):
                            ready = (lambda k: pe.wait_ge(xg_ready, l * N_X + 2 * KT + k + 1)) if first and s == 0 else None
                            tile(base + j * 4 + piece0, tile0 + j * 2 + (first_tile + s),
                                 [(2 * s, 0, 8), (2 * s + 1, 8, 8)], act_a, gemm[s % 2], ready)
                            if first and s == 0:
                                statistic(l, ST_X3)

                    quad(0, first=c == 0)
                    with pe.Fori(1, FT // 2) as jq:
                        quad(jq * 2)
                    with pe.Fori(0, KT // 4) as j:
                        for s in range(4):
                            ready = (lambda k: pe.wait_ge(h_ready, l * (FF_CHUNKS * FT) + (c * FT + (FT - 2 if k == 0 else FT)))
                                     if k in (0, FT - 2) else None) if s == 0 else None
                            tile(base + j * 12 + (piece0 + 4 * FT), tile0 + j * 4 + (first_tile + 2 * FT + s),
                                 [(3 * s + k, 8 * k, DN_PIECES[k]) for k in range(3)], act_h, gemm[s % 2], ready)
            statistic(DEPTH, ST_X1)


def tiles_of(w, cols):
    k = w.shape[0] // P
    w = w.reshape(k, P, w.shape[1])
    out = np.empty((len(cols), P, k, P), w.dtype)
    for n, c in enumerate(cols):
        out[n] = w[:, :, c].transpose(1, 0, 2)
    return out.reshape(len(cols), P, k * P)


def window_heads():
    return [np.r_[j * HD:(j + 1) * HD, (j + 4) * HD:(j + 5) * HD] for j in range(4)]


def win_columns():
    block = lambda at: [np.arange(at + j * P, at + (j + 1) * P) for j in range(4)]
    qa, ka, va, qb, kb, vb, qc, kc, vc, ud = 0, 512, 1024, 1536, 2048, 2176, 2304, 2816, 3328, 3840
    value, gate = block(ud), block(ud + GROUP)
    cols = [t for pair in zip(gate, value) for t in pair]
    cols += block(qa) + block(ka) + block(va)
    cols += [qb + w for w in window_heads()] + [np.arange(kb, kb + P), np.arange(vb, vb + P)]
    return cols + block(qc) + block(kc) + block(vc)


def feature_major(v):
    return np.swapaxes(v.reshape(*v.shape[:-1], -1, P), -1, -2)


def constants():
    c = np.zeros((P, NCONST), np.float32)
    i = np.arange(P)
    c[:, K_ID:K_ID + P] = np.eye(P)
    c[:, K_TRI:K_TRI + P] = i[:, None] > i[None, :]
    c[:, K_ONE:K_ONE + P] = 1.0
    half = HD // 2
    for m in range(P):
        if m % HD < half:
            c[m + half, K_ROT + m] = -1.0
        else:
            c[m - half, K_ROT + m] = 1.0
    c[:, K_MSK:K_MSK + P] = i[:, None] < i[None, :]
    c[:, K_INV] = np.float32(10000.0) ** (-(i % half).astype(np.float32) / np.float32(half))
    return c


def kernel(**inputs):
    import concourse.bacc as bacc
    from concourse.bass_utils import run_bass_kernel_spmd

    v = {k: np.asarray(w) for k, w in inputs.items()}
    L = DEPTH
    heads = window_heads()
    order = np.concatenate([np.arange(GROUP)] + [GROUP + h for h in heads] + [np.arange(3 * GROUP, 4 * GROUP), np.arange(2 * GROUP, 3 * GROUP)])
    block = [np.arange(j * P, (j + 1) * P) for j in range(D_FF // P * 2)]

    arrays = {}
    arrays["x"] = v["x"][0].T.reshape(KT, P, SEQ).transpose(1, 0, 2)
    arrays["mem"] = v["mem"][0].T.reshape(KT, P, N_MEM).transpose(1, 0, 2)
    arrays["pos"] = np.broadcast_to(v["positions"].astype(np.int32), (P, SEQ))
    const = constants()
    const[:, K_G0:K_G0 + KT] = feature_major(v["norm_mix_g"][0])
    const[:, K_GF:K_GF + KT] = feature_major(v["final_norm_g"])
    arrays["const"] = const

    par = np.zeros((L, P, NPAR), np.float32)
    par[:, :, C_XG:C_XG + KT] = feature_major(v["norm_xattn_g"])
    par[:, :, C_MG:C_MG + KT] = feature_major(v["norm_mem_g"])
    par[:, :, C_FG:C_FG + KT] = feature_major(v["norm_ffn_g"])
    for l in range(L):
        par[l, :, C_AG:C_AG + KT] = feature_major(v["norm_mix_g"][l + 1] if l + 1 < L else v["final_norm_g"])
    par[:, :, C_GG:C_GG + KT] = feature_major(v["group_norm_g"][:, order])
    par[:, :, C_DW:C_DB] = v["conv_dw_w"].reshape(L, CONV_WIDTH, GT, P).transpose(0, 3, 2, 1).reshape(L, P, -1)
    for c, name in ((C_DB, "conv_dw_b"), (C_LG, "conv_ln_g"), (C_LB, "conv_ln_b"), (C_PB, "conv_pw_b")):
        par[:, :, c:c + GT] = feature_major(v[name])
    for j in range(4):
        for c in range(4):
            par[:, :, C_SK + 4 * j + c] = v["swa_sinks"][:, j + 4 * (c % 2)][:, None]
    arrays["par"] = par

    q, k = np.arange(P)[:, None], np.arange(2 * P)[None, :] - P
    later = k // HD > q // HD
    index = np.clip(q - k, -MAX_REL, MAX_REL) + MAX_REL
    rel = v["ca_rel_bias"][:, :, index]
    rel[:, :, later] = NEG
    arrays["bias"] = rel.reshape(L, 4, 2, P, 2 * P).transpose(0, 1, 3, 2, 4)
    window = np.where(later | (k // HD < q // HD - 1), np.float32(NEG), np.float32(0))
    arrays["win_mask"] = np.stack([window, window], 1)

    win = win_columns()
    arrays["w_main"] = np.stack([np.concatenate([tiles_of(v["w_in"][l], win), tiles_of(v["w_xkv"][l], block[:8])])
                                 for l in range(L)])
    arrays["w_next"] = arrays["w_main"][[(l + 1) % L for l in range(L)], 0]
    arrays["w_pw"] = np.stack([tiles_of(v["conv_pw_w"][l], block[:4]) for l in range(L)])
    arrays["w_out"] = np.stack([tiles_of(v["w_out"][l][order], block[:16]) for l in range(L)])
    arrays["w_xq"] = np.stack([tiles_of(v["w_xq"][l], block[:4]) for l in range(L)])
    arrays["w_xo"] = np.stack([tiles_of(v["w_xo"][l], block[:16]) for l in range(L)])
    nf = D_FF // P
    gu = [c for j in range(nf) for c in (block[j], block[nf + j])]
    arrays["w_gu"] = np.stack([tiles_of(v["w_gate_up"][l], gu) for l in range(L)])\
        .reshape(L, FF_CHUNKS, 2 * FT, P, KT * P)
    arrays["w_dn"] = np.stack([[tiles_of(v["w_down"][l][c * FT * P:(c + 1) * FT * P], block[:16])
                                for c in range(FF_CHUNKS)] for l in range(L)])

    nc = bacc.Bacc("TRN2", target_bir_lowering=False, num_devices=1)
    args = {}
    for name in list(arrays):
        arr = np.ascontiguousarray(arrays.pop(name))
        arrays[f"in_{name}"] = arr
        args[name] = nc.dram_tensor(f"in_{name}", arr.shape, mybir.dt.from_np(arr.dtype), kind="ExternalInput").ap()
    args["out"] = nc.dram_tensor("out", (P, KT, SEQ), F32, kind="ExternalOutput").ap()
    build(nc, args)
    r = run_bass_kernel_spmd(nc, [arrays], core_ids=[0])
    out = np.asarray(r.results[0]["out"])
    return np.ascontiguousarray(out.transpose(2, 1, 0).reshape(1, SEQ, D_MODEL))
```
